# Optimizing a Trainium2 kernel written in Bass

```python
import math
import jax, jax.numpy as jnp
from jax import lax
import numpy as np

D_MODEL = 4096
BATCH = 1
SEQ = 256
DEPTH = 1

MLA_HEADS = 16
Q_LORA_RANK = 1024
KV_LORA_RANK = 512
QK_NOPE_DIM = 128
QK_ROPE_DIM = 64
QK_HEAD_DIM = QK_NOPE_DIM + QK_ROPE_DIM
V_HEAD_DIM = 128
MLA_WIDTH = MLA_HEADS * V_HEAD_DIM
ROPE_THETA = 10000.0
Q_BLOCK = 128

DIL_GROUPS = ((128, 1), (512, 4), (2048, 16))
N_DIL_GROUPS = 3
DSWA_HEADS_PER_GROUP = 8
DSWA_HEADS = N_DIL_GROUPS * DSWA_HEADS_PER_GROUP
DSWA_HEAD_DIM = 128
DSWA_QKV_WIDTH = DSWA_HEADS * DSWA_HEAD_DIM
DSWA_WIDTH = DSWA_HEADS_PER_GROUP * DSWA_HEAD_DIM

REL_BUCKETS = 32
REL_MAX_DISTANCE = 1024

DEEPNORM_ALPHA = (2.0 * DEPTH) ** 0.25
DEEPNORM_BETA = (8.0 * DEPTH) ** -0.25
LN_EPS = 1e-5
RMS_EPS = 1e-6
NEG_INF = -1e30

IN_SPLITS = (
    Q_LORA_RANK,
    KV_LORA_RANK + QK_ROPE_DIM,
    DSWA_QKV_WIDTH,
    DSWA_QKV_WIDTH,
    DSWA_QKV_WIDTH,
    MLA_WIDTH,
    DSWA_WIDTH,
    D_MODEL,
    D_MODEL,
)
IN_WIDTH = sum(IN_SPLITS)
IN_OFFSETS = tuple(int(v) for v in np.cumsum(IN_SPLITS)[:-1])
DSWA_V_START = IN_OFFSETS[3]
DSWA_V_END = IN_OFFSETS[4]

kernel_name = "hybrid_mla_dilated_window_encoder_layer"

def layer_norm(x, g, b):
    xf = x.astype(jnp.float32)
    mu = jnp.mean(xf, axis=-1, keepdims=True)
    xc = xf - mu
    var = jnp.mean(xc * xc, axis=-1, keepdims=True)
    return (xc * lax.rsqrt(var + LN_EPS) * g.astype(jnp.float32) + b.astype(jnp.float32)).astype(x.dtype)

def rms_norm(x, g):
    xf = x.astype(jnp.float32)
    y = xf * lax.rsqrt(jnp.mean(xf * xf, axis=-1, keepdims=True) + RMS_EPS)
    return (y * g.astype(jnp.float32)).astype(x.dtype)

def rope(t, cos, sin):
    half = t.shape[-1] // 2
    t1 = t[..., :half].astype(jnp.float32)
    t2 = t[..., half:].astype(jnp.float32)
    return jnp.concatenate([t1 * cos - t2 * sin, t2 * cos + t1 * sin], axis=-1).astype(t.dtype)

def t5_bucket(rel):
    nb = REL_BUCKETS // 2
    max_exact = nb // 2
    n = jnp.abs(rel)
    nf = jnp.maximum(n, 1).astype(jnp.float32)
    large = max_exact + (jnp.log(nf / max_exact) / math.log(REL_MAX_DISTANCE / max_exact)
                         * (nb - max_exact)).astype(jnp.int32)
    large = jnp.minimum(large, nb - 1)
    return jnp.where(rel > 0, nb, 0) + jnp.where(n < max_exact, n, large)

def mla_attention(q_a, kv_a, q_a_norm_g, w_q_b, kv_a_norm_g, w_kv_b):
    B, S, _ = q_a.shape
    q = (rms_norm(q_a, q_a_norm_g) @ w_q_b).reshape(B, S, MLA_HEADS, QK_HEAD_DIM)
    q_nope, q_pe = q[..., :QK_NOPE_DIM], q[..., QK_NOPE_DIM:]
    c_kv, k_pe = kv_a[..., :KV_LORA_RANK], kv_a[..., KV_LORA_RANK:]
    kv = (rms_norm(c_kv, kv_a_norm_g) @ w_kv_b).reshape(B, S, MLA_HEADS, QK_NOPE_DIM + V_HEAD_DIM)
    k_nope, v = kv[..., :QK_NOPE_DIM], kv[..., QK_NOPE_DIM:]

    pos = jnp.arange(S, dtype=jnp.float32)
    inv_freq = 1.0 / (ROPE_THETA ** (jnp.arange(0, QK_ROPE_DIM, 2, dtype=jnp.float32) / QK_ROPE_DIM))
    ang = pos[:, None] * inv_freq[None, :]
    cos, sin = jnp.cos(ang), jnp.sin(ang)
    q_pe = rope(q_pe, cos[None, :, None, :], sin[None, :, None, :])
    k_pe = rope(k_pe, cos[None], sin[None])

    scale = QK_HEAD_DIM ** -0.5
    n_blk = S // Q_BLOCK

    def to_blocks(t):
        return jnp.moveaxis(t.reshape(B, n_blk, Q_BLOCK, t.shape[2], t.shape[3]), 1, 0)

    def attend(blk):
        qn_b, qp_b = blk
        s = (jnp.einsum('bqhd,bkhd->bhqk', qn_b, k_nope)
             + jnp.einsum('bqhd,bkd->bhqk', qp_b, k_pe)).astype(jnp.float32) * scale
        p = jax.nn.softmax(s, axis=-1)
        return jnp.einsum('bhqk,bkhd->bqhd', p.astype(v.dtype), v)

    o = lax.map(attend, (to_blocks(q_nope), to_blocks(q_pe)))
    return jnp.moveaxis(o, 0, 1).reshape(B, S, MLA_WIDTH)

def dilated_band_attention(q, k, v, bias_tab, window, dil):
    B, S, H, Dh = q.shape
    half = window // (2 * dil)
    L = -(-S // (half * dil)) * half
    nb = L // half
    Sp = L * dil
    pad = ((0, 0), (0, Sp - S), (0, 0), (0, 0))

    def to_res(t):
        return jnp.pad(t, pad).reshape(B, L, dil, H, Dh).transpose(0, 2, 1, 3, 4)

    def band(t):
        widths = [(0, 0), (0, 0), (half, half)] + [(0, 0)] * (t.ndim - 3)
        tb = jnp.pad(t, widths).reshape(t.shape[:2] + (nb + 2, half) + t.shape[3:])
        return jnp.concatenate([tb[:, :, :-2], tb[:, :, 1:-1], tb[:, :, 2:]], axis=3)

    qr = to_res(q).reshape(B, dil, nb, half, H, Dh)
    kb = band(to_res(k))
    vb = band(to_res(v))
    valid = (jnp.arange(Sp) < S).reshape(L, dil).T[None]
    kvalid = band(valid)

    steps = jnp.arange(3 * half)[None, :] - half - jnp.arange(half)[:, None]
    in_band = jnp.abs(steps) <= half
    bias = jnp.transpose(bias_tab[t5_bucket(steps * dil)], (2, 0, 1)).astype(jnp.float32)

    s = jnp.einsum('brnqhd,brnkhd->brnhqk', qr, kb).astype(jnp.float32) * (Dh ** -0.5) + bias
    mask = in_band & kvalid[:, :, :, None, None, :]
    s = jnp.where(mask, s, NEG_INF)
    m = jnp.max(s, axis=-1, keepdims=True)
    p = jnp.exp(s - m)
    den = jnp.sum(p, axis=-1, keepdims=True)
    o = jnp.einsum('brnhqk,brnkhd->brnqhd', (p / den).astype(v.dtype), vb)
    lse = (m + jnp.log(den))[..., 0]

    o = o.reshape(B, dil, L, H, Dh).transpose(0, 2, 1, 3, 4).reshape(B, Sp, H, Dh)[:, :S]
    lse = lse.transpose(0, 1, 2, 4, 3).reshape(B, dil, L, H).transpose(0, 2, 1, 3).reshape(B, Sp, H)[:, :S]
    return o, lse

def dilated_mixture(dq, dk, dv, rel_bias):
    B, S, _ = dq.shape
    q = dq.reshape(B, S, DSWA_HEADS, DSWA_HEAD_DIM)
    k = dk.reshape(B, S, DSWA_HEADS, DSWA_HEAD_DIM)
    v = dv.reshape(B, S, DSWA_HEADS, DSWA_HEAD_DIM)
    outs, lses = [], []
    for g, (window, dil) in enumerate(DIL_GROUPS):
        hs = slice(g * DSWA_HEADS_PER_GROUP, (g + 1) * DSWA_HEADS_PER_GROUP)
        o, lse = dilated_band_attention(q[:, :, hs], k[:, :, hs], v[:, :, hs], rel_bias[:, hs], window, dil)
        outs.append(o)
        lses.append(lse)
    w = jax.nn.softmax(jnp.stack(lses, axis=0), axis=0)
    mix = jnp.sum(w[..., None] * jnp.stack(outs, axis=0).astype(jnp.float32), axis=0)
    return mix.astype(dq.dtype).reshape(B, S, DSWA_WIDTH)

def setup_inputs(seed: int = 0) -> dict:
    key = jax.random.key(seed)
    ks = jax.random.split(key, 16)
    f32 = jnp.float32
    x = jax.random.normal(ks[0], (BATCH, SEQ, D_MODEL), f32)
    emb_ln_g = 1.0 + 0.02 * jax.random.normal(ks[1], (D_MODEL,), f32)
    emb_ln_b = 0.02 * jax.random.normal(ks[2], (D_MODEL,), f32)
    rel_bias = 0.5 * jax.random.normal(ks[3], (REL_BUCKETS, DSWA_HEADS), f32)
    col_scale = jnp.ones((IN_WIDTH,), f32).at[DSWA_V_START:DSWA_V_END].set(DEEPNORM_BETA)
    w_in = jax.random.normal(ks[4], (DEPTH, D_MODEL, IN_WIDTH), f32) * (D_MODEL ** -0.5) * col_scale
    q_a_norm_g = 1.0 + 0.02 * jax.random.normal(ks[5], (DEPTH, Q_LORA_RANK), f32)
    w_q_b = jax.random.normal(ks[6], (DEPTH, Q_LORA_RANK, MLA_HEADS * QK_HEAD_DIM), f32) * (Q_LORA_RANK ** -0.5)
    kv_a_norm_g = 1.0 + 0.02 * jax.random.normal(ks[7], (DEPTH, KV_LORA_RANK), f32)
    kv_col_scale = jnp.tile(jnp.concatenate([jnp.ones((QK_NOPE_DIM,), f32),
                                             jnp.full((V_HEAD_DIM,), DEEPNORM_BETA, f32)]), MLA_HEADS)
    w_kv_b = (jax.random.normal(ks[8], (DEPTH, KV_LORA_RANK, MLA_HEADS * (QK_NOPE_DIM + V_HEAD_DIM)), f32)
              * (KV_LORA_RANK ** -0.5) * kv_col_scale)
    w_o_mla = jax.random.normal(ks[9], (DEPTH, MLA_WIDTH, D_MODEL), f32) * (MLA_WIDTH ** -0.5) * DEEPNORM_BETA
    w_o_dswa = jax.random.normal(ks[10], (DEPTH, DSWA_WIDTH, D_MODEL), f32) * (DSWA_WIDTH ** -0.5) * DEEPNORM_BETA
    w_out = jax.random.normal(ks[11], (DEPTH, D_MODEL, D_MODEL), f32) * (D_MODEL ** -0.5) * DEEPNORM_BETA
    ln_g = 1.0 + 0.02 * jax.random.normal(ks[12], (DEPTH, D_MODEL), f32)
    ln_b = 0.02 * jax.random.normal(ks[13], (DEPTH, D_MODEL), f32)
    return {"x": x, "emb_ln_g": emb_ln_g, "emb_ln_b": emb_ln_b, "rel_bias": rel_bias,
            "w_in": w_in, "q_a_norm_g": q_a_norm_g, "w_q_b": w_q_b, "kv_a_norm_g": kv_a_norm_g,
            "w_kv_b": w_kv_b, "w_o_mla": w_o_mla, "w_o_dswa": w_o_dswa, "w_out": w_out,
            "ln_g": ln_g, "ln_b": ln_b}

def reference(x, emb_ln_g, emb_ln_b, rel_bias, w_in, q_a_norm_g, w_q_b, kv_a_norm_g,
              w_kv_b, w_o_mla, w_o_dswa, w_out, ln_g, ln_b):
    h = layer_norm(x, emb_ln_g, emb_ln_b)
    for l in range(DEPTH):
        proj = h @ w_in[l]
        q_a, kv_a, dq, dk, dv, g_mla, g_dswa, r_mla, r_dswa = jnp.split(proj, IN_OFFSETS, axis=-1)
        a = mla_attention(q_a, kv_a, q_a_norm_g[l], w_q_b[l], kv_a_norm_g[l], w_kv_b[l])
        y_mla = (a * jax.nn.silu(g_mla)) @ w_o_mla[l]
        b = dilated_mixture(dq, dk, dv, rel_bias)
        y_dswa = (b * jax.nn.silu(g_dswa)) @ w_o_dswa[l]
        merged = jax.nn.sigmoid(r_mla) * y_mla + jax.nn.sigmoid(r_dswa) * y_dswa
        out = merged @ w_out[l]
        h = layer_norm(DEEPNORM_ALPHA * h + out, ln_g[l], ln_b[l])
    return h


_drawn_inputs = setup_inputs


def setup_inputs(seed=0):
    import zlib

    import numpy as np

    out = dict(_drawn_inputs(seed))
    spreads = {}
    factors = {'emb_ln_g': 2.775,
     'emb_ln_b': 2.823,
     'rel_bias': 8.0,
     'w_in': 4.713,
     'q_a_norm_g': 8.0,
     'w_q_b': 8.0,
     'kv_a_norm_g': 8.0,
     'w_kv_b': 7.679,
     'w_o_mla': 8.0,
     'w_o_dswa': 7.627,
     'w_out': 5.752,
     'ln_g': 2.875,
     'ln_b': 2.879}
    for name, (base, spread) in spreads.items():
        noise = np.random.default_rng([zlib.crc32(name.encode()), seed]).standard_normal(out[name].shape)
        drawn = base * np.exp(spread * noise) if base else spread * noise
        out[name] = __import__('jax').numpy.asarray(drawn.astype(out[name].dtype))
    for name, factor in factors.items():
        out[name] = (out[name] * factor).astype(out[name].dtype)
    return out
```

```python
import numpy as np
from contextlib import ExitStack, contextmanager
import concourse.bass as bass
from concourse import mybir

F32 = mybir.dt.float32
F32R = mybir.dt.float32r
ALU = mybir.AluOpType
ACT = mybir.ActivationFunctionType
AX = mybir.AxisListType

P = 128
D = 4096
SEQ = 256
TT = SEQ // P
Q_RANK, KV_RANK = 1024, 512
MLA_HEADS, NOPE, ROPE, HD = 16, 128, 64, 128
QHD = NOPE + ROPE
MLA_W = MLA_HEADS * HD
GROUPS = ((128, 1), (512, 4), (2048, 16))
NG, GH = len(GROUPS), 8
DS_W = GH * HD
QKV_W = NG * DS_W
BUCKETS, MAX_DIST = 32, 1024
ALPHA = 2.0 ** 0.25
LN_EPS, RMS_EPS, NEG = 1e-5, 1e-6, -1e30
MLA_SCALE, DS_SCALE = QHD ** -0.5, HD ** -0.5
COL_QA = 0
COL_KVA = COL_QA + Q_RANK
COL_DQ = COL_KVA + KV_RANK + ROPE
COL_DK = COL_DQ + QKV_W
COL_DV = COL_DK + QKV_W
COL_GM = COL_DV + QKV_W
COL_GD = COL_GM + MLA_W
COL_RM = COL_GD + DS_W
COL_RD = COL_RM + D

RES, LEN = 4, SEQ // 4
NDR, NDL = 2 * RES - 1, 2 * LEN - 1
ROWLEN = NDR * NDL
PITCH = 896

CW = 512
RING = 4
AHEAD = 3
KT = D // P
QUAD = CW // HD
UNIT_Q = 2 * QHD


def positions():
    t, p = np.meshgrid(np.arange(TT), np.arange(P), indexing="ij")
    return 4 * (p % LEN) + 2 * t + p // LEN


def rope_table():
    inv = np.float32(1.0) / (np.float32(10000.0) ** (np.arange(0, ROPE, 2, dtype=np.float32) / np.float32(ROPE)))
    ang = (positions().astype(np.float32)[:, :, None] * inv[None, None, :].astype(np.float32)).astype(np.float32)
    cos, sin = np.cos(ang.astype(np.float64)), np.sin(ang.astype(np.float64))
    both = np.stack([np.concatenate([cos, cos], -1), np.concatenate([-sin, sin], -1)], 0)
    return np.ascontiguousarray(both.transpose(2, 0, 1, 3).astype(np.float32))


def bucket_table():
    dr, dl = np.meshgrid(np.arange(NDR) - (RES - 1), np.arange(NDL) - (LEN - 1), indexing="ij")
    rel = (RES * dl + dr).reshape(-1)
    nb = BUCKETS // 2
    exact = nb // 2
    n = np.abs(rel)
    large = exact + (np.log(np.maximum(n, 1) / exact) / np.log(MAX_DIST / exact) * (nb - exact)).astype(np.int64)
    b = np.where(rel > 0, nb, 0) + np.where(n < exact, n, np.minimum(large, nb - 1))
    table = np.zeros((BUCKETS + NG, rel.size), np.float32)
    table[b, np.arange(rel.size)] = 1.0
    for g, (window, dil) in enumerate(GROUPS):
        ok = (n % dil == 0) & (n <= window // 2)
        table[BUCKETS + g] = np.where(ok, 0.0, NEG)
    return table


class Chunk:

    def __init__(self, w, col, per, left, slots, kt, width, side):
        self.w, self.col, self.per, self.left = w, col, per, left
        self.slots, self.kt, self.width, self.side = slots, kt, width, side


class Section:

    def __init__(self, name, turns, chunks):
        self.name, self.turns, self.chunks = name, turns, chunks
        self.per_slot, self.per_chunk = sum(c.slots for c in chunks), len(chunks)


def sections():
    def full(col, per, side, w="in"):
        return Chunk(w, col, per, "h", KT // 2, 2, CW, side)

    def unit(u, per, side):
        return [Chunk("qb", UNIT_Q * u, per * UNIT_Q, "qa", 4, 2, UNIT_Q, side),
                Chunk("kvb", CW * u, per * CW, "kva", 4, 1, CW, side + "_kv")]

    half = (KV_RANK + ROPE) // 2
    body = []
    for g in range(NG):
        c = g * DS_W
        if g:
            body.append(full(COL_DQ + c, CW, f"att{g - 1}"))
        body.append(full(COL_DK + c, CW, f"qT{g}"))
        body.append(full(COL_DV + c, CW, f"kT{g}"))
    body.append(full(COL_GD, CW, f"att{NG - 1}"))
    body.append(full(COL_DQ + CW, COL_RM - (COL_DQ + CW), "mix"))
    out = [
        Section("start", None,
                [Chunk("in", COL_KVA + half * n, 0, "h", KT // 2, 2, half, s) for n, s in ((0, "hT"), (1, "kva0"))]
                + [full(COL_QA, 0, "kva1"), full(COL_QA + CW, 0, "qa0"), full(COL_GM, 0, "qa1")]
                + [full(COL_GM + CW * n, 0, f"gm{n - 1}") for n in (1, 2, 3)]),
        Section("unit0", None, unit(0, 0, "gm3")),
        Section("mla", 6, unit(1, 1, "mla")),
        Section("mla7", None, unit(7, 0, "mla")),
        Section("dq0", None, [full(COL_DQ, 0, "mla_last")]),
        Section("dswa", 2, body),
        Section("merge", 7, [
            full(COL_RD, CW, "rm"),
            Chunk("om", 0, CW, "am", 8, 2, CW, "rd"),
            Chunk("od", 0, CW, "b", 4, 2, CW, "ym"),
            full(COL_RM + CW, CW, "yd")]),
        Section("merge7", None, [
            full(COL_RD + 7 * CW, 0, "rm"),
            Chunk("om", 7 * CW, 0, "am", 8, 2, CW, "rd_split"),
            Chunk("od", 7 * CW, 0, "b", 4, 2, CW, "ym")]),
        Section("out0", None, [full(0, 0, "yd_last", "out")]),
        Section("out", 3, [full(CW, 2 * CW, "fin0", "out"), full(2 * CW, 2 * CW, "fin1", "out")]),
        Section("out7", None, [full(7 * CW, 0, "fin6", "out")]),
    ]
    slot = chunk = 0
    for s in out:
        s.slot0, s.chunk0 = slot, chunk
        slot += s.per_slot * (s.turns or 1)
        chunk += s.per_chunk * (s.turns or 1)
        assert s.slot0 % RING == 0 and s.per_slot % RING == 0
        assert s.turns is None or s.per_chunk % 2 == 0
    return out, slot, chunk


SECTIONS, NSLOTS, NCHUNKS = sections()
SEC = {s.name: s for s in SECTIONS}


def at(i, per, base):
    return base if i is None else i * per + base


@contextmanager
def turns(engine, section):
    if section.turns is None:
        yield None
    else:
        with engine.Fori(0, section.turns) as i:
            yield i


def slots_of(section):
    n = 0
    for ci, c in enumerate(section.chunks):
        for j in range(c.slots):
            yield c, ci, j, n
            n += 1


class Steps:

    def __init__(self, engine, sem):
        self.engine, self.sem, self.n, self.i, self.per = engine, sem, 0, None, 0

    def enter(self, i, per):
        self.i, self.per, self.base = i, per, self.n

    def leave(self, turns_):
        if self.i is not None:
            assert self.n - self.base == self.per, (self.sem, self.n - self.base)
            self.n = self.base + self.per * turns_
            self.i = None

    def done(self, ins):
        ins.then_inc(self.sem, 1)
        self.n += 1

    def wait(self):
        self.engine.wait_ge(self.sem, at(self.i, self.per, self.n))


VECTOR_STEPS = {"mla": 3, "dswa": 38, "merge": 2, "out": 2}
POOL_STEPS = {"mla": 2}
END_VECTOR, END_POOL = (0, 1, 2, 3, 4), (5, 6, 7)


def bias_dmas(head):
    return 2 * TT if head < QUAD else 2


def bias_arrivals(head):
    return 16 * sum(bias_dmas(n) for n in range(head + 1) if n % 2 == head % 2)


def program(nc, x, emb_g, emb_b, rel_bias, w_in, qa_g, w_qb, kva_g, w_kvb, w_om, w_od, w_out, ln_g, ln_b, out):
    ident_c = nc.inline_tensor(np.eye(P, dtype=np.float32), name="identity_const").ap()
    rope_c = nc.inline_tensor(rope_table(), name="rope_const").ap()
    bucket_c = nc.inline_tensor(bucket_table(), name="bucket_const").ap()
    group_c = nc.inline_tensor(np.repeat(np.eye(NG, dtype=np.float32), GH, axis=1), name="group_const").ap()
    bias_rows_d = nc.dram_tensor("bias_rows", (NG * GH, LEN, PITCH), F32).ap()

    with ExitStack() as ctx:
        K = 1024
        base = (nc.sbuf_base + 31) // 32 * 32
        OPER = base
        RINGS = OPER + 64 * K
        R_A = RINGS + 48 * K
        R_B = R_A + 32 * K
        R_C = R_B + 16 * K
        SMALL = R_C + 32 * K

        def sb(name, at_, shape, dt=F32):
            return nc.alloc_sbuf_tensor_at(name, shape, dt, offset=at_).ap()

        oper_hi = sb("oper_hi", OPER, [P, KT, SEQ], F32R)
        oper_lo = sb("oper_lo", OPER + 32 * K, [P, KT, SEQ], F32R)
        w_raw = sb("w_raw", RINGS, [P, RING, 2 * CW])
        w_hi = sb("w_hi", RINGS + 16 * K, [P, RING, 2 * CW], F32R)
        w_lo = sb("w_lo", RINGS + 32 * K, [P, RING, 2 * CW], F32R)
        x_sb = sb("x_sb", R_A, [P, TT, D])
        am_hi = sb("am_hi", R_A, [P, MLA_HEADS, SEQ], F32R)
        am_lo = sb("am_lo", R_A + 16 * K, [P, MLA_HEADS, SEQ], F32R)
        resid = sb("resid", R_A, [P, TT, D])
        bucket_sb = sb("bucket_sb", R_B, [BUCKETS + NG, ROWLEN])
        rowsb = sb("rowsb", R_B + 4 * K, [NG * GH, PITCH])
        relb = sb("relb", R_B + 8 * K, [BUCKETS + NG, NG * GH])
        qa_hi = sb("qa_hi", R_B, [P, Q_RANK // P, SEQ], F32R)
        qa_lo = sb("qa_lo", R_B + 8 * K, [P, Q_RANK // P, SEQ], F32R)
        b_hi = sb("b_hi", R_B, [P, GH, SEQ], F32R)
        b_lo = sb("b_lo", R_B + 8 * K, [P, GH, SEQ], F32R)
        ln_g_row = sb("ln_g_row", R_B, [P, D])
        h_val = sb("h_val", R_C, [P, 4, SEQ])
        gm_sb = sb("gm_sb", R_C, [P, TT, MLA_W])
        kva_hi = sb("kva_hi", R_C + 16 * K, [P, KV_RANK // P, SEQ], F32R)
        kva_lo = sb("kva_lo", R_C + 20 * K, [P, KV_RANK // P, SEQ], F32R)
        qa_sb = sb("qa_sb", R_C + 24 * K, [P, TT, Q_RANK])
        q_sb = sb("q_sb", R_C + 24 * K, [P, TT, 2, QHD])
        v_sb = sb("v_sb", R_C + 27 * K, [P, TT, 2, HD])
        qnT = sb("qnT", R_C + 29 * K, [P, 2, SEQ])
        a_sb = sb("a_sb", R_C, [P, TT, CW])
        dv_sb = sb("dv_sb", R_C + 4 * K, [P, TT, CW])
        dqT = sb("dqT", R_C + 8 * K, [P, QUAD, SEQ])
        dkT = sb("dkT", R_C + 12 * K, [P, QUAD, SEQ])
        o_sb = sb("o_sb", R_C + 16 * K, [P, NG, TT, QUAD, HD])
        gate_sb = sb("gate_sb", R_C + 28 * K, [P, TT, CW])
        mT = sb("mT", R_C, [P, KT, SEQ])
        emb_g_row = sb("emb_g_row", R_C, [P, D])
        emb_b_row = sb("emb_b_row", R_C + 16 * K, [P, D])
        ln_b_row = sb("ln_b_row", R_C, [P, D])
        o = SMALL
        ident = sb("ident", o, [P, P])
        rope_sb = sb("rope_sb", o + 512, [P, 2, TT, ROPE])
        kpeT = sb("kpeT", o + 1536, [ROPE, SEQ])
        NV = 2 * KT + Q_RANK // P + KV_RANK // P
        gains = sb("gains", o + 2560, [P, NV])
        stat = sb("stat", o + 2880, [P, 16])
        pair = sb("pair", o + 3264, [P, TT, 2])
        m_sb = sb("m_sb", o + 2944, [P, NG, TT * QUAD])
        den_sb = sb("den_sb", o + 3040, [P, NG, TT * QUAD])
        big_m = sb("big_m", o + 3136, [P, TT * QUAD])
        wgt = sb("wgt", o + 3168, [P, NG, TT * QUAD])
        TAIL = o + 3296
        vecs = sb("vecs", TAIL, [NV, P])
        bn = sb("bn", TAIL + 512, [P, TT, D // CW, 6])
        kva_sb = sb("kva_sb", TAIL + 1024, [P, TT, KV_RANK + ROPE])
        ropet = sb("ropet", TAIL + 6 * K, [P, TT, ROPE])
        junk = sb("junk", TAIL + 7 * K, [P, Q_RANK])
        n_val = sb("n_val", TAIL + 7 * K, [P, 4, SEQ])
        knT = sb("knT", TAIL, [P, 2, SEQ])
        gated = sb("gated", TAIL, [P, TT, 2, HD])
        qpT = sb("qpT", TAIL + 2 * K, [ROPE, 2, SEQ])
        probs = sb("probs", TAIL + 4 * K, [P, 2, TT, SEQ])
        k_sb = sb("k_sb", TAIL + 4 * K, [P, TT, 2, HD])
        probsT = sb("probsT", TAIL + 8 * K, [P, 2, TT, SEQ])
        qrope = sb("qrope", R_C + 31 * K, [P, TT, 2, ROPE])
        bias_sb = sb("bias_sb", TAIL, [P, 2, TT * SEQ])
        s_sb = sb("s_sb", TAIL + 4 * K, [P, TT * SEQ])
        dprobs = sb("dprobs", TAIL + 6 * K, [P, TT * SEQ])
        dprobsT = sb("dprobsT", TAIL + 8 * K, [P, TT * SEQ])
        sig_m = sb("sig_m", TAIL, [P, TT, CW])
        sig_d = sb("sig_d", TAIL + 4 * K, [P, TT, CW])
        ym = sb("ym", TAIL + 8 * K, [P, TT, CW])
        xbn = sb("xbn", TAIL, [P, TT, D // CW, 6])
        ybn = sb("ybn", TAIL + 512, [P, TT, D // CW, 6])
        assert TAIL + 12 * K <= nc.sbuf_usable_end, (TAIL + 12 * K, nc.sbuf_usable_end)

        acc = [ctx.enter_context(nc.psum_tensor(f"acc{n}", [P, TT, CW], F32)) for n in range(2)]
        BK = [ctx.enter_context(nc.psum_tensor(f"bank{n}", [P, CW], F32)) for n in range(4)]
        bA, bB, bC, bD = BK

        def sem(name):
            return ctx.enter_context(nc.semaphore(name))

        w_loaded = [sem(f"w_loaded{n}") for n in range(RING)]
        w_hi_ready, w_lo_ready, slot_done, acc_free = (sem(n) for n in ("w_hi_ready", "w_lo_ready", "slot_done", "acc_free"))
        x_loaded = [sem(f"x_loaded{t}") for t in range(TT)]
        consts_loaded, bias_in = sem("consts_loaded"), sem("bias_in")
        vector_step, pool_step, sqrt_ready, var_ready = (sem(n) for n in ("vector_step", "pool_step", "sqrt_ready", "var_ready"))
        gains_ps, gains_ready = sem("gains_ps"), sem("gains_ready")
        z_ready, hT_ps, hT_hi, hT_val, hT_lo = (sem(n) for n in ("z_ready", "hT_ps", "hT_hi", "hT_val", "hT_lo"))
        rows_ps, rows_ready, rows_ready2, rows_stored = (sem(n) for n in ("rows_ps", "rows_ready", "rows_ready2", "rows_stored"))
        sumsq_ready, normed, nT_ps, nT_hi, nT_val, nT_lo = (sem(n) for n in ("sumsq_ready", "normed", "nT_ps", "nT_hi", "nT_val", "nT_lo"))
        kpe_roped, kpe_ps, kpeT_ready = sem("kpe_roped"), sem("kpe_ps"), sem("kpeT_ready")
        gate_exp = sem("gate_exp")
        (q_evac, q_roped, qnT_ps, qpT_ps, knT_ps, qnT_ready, qpT_ready, knT_ready, scores, negmax, probs_ready,
         probsT_ps, probsT0, probsT1, o_ps, gated_ready, gT_ps, am_hi_ready, am_lo_ready) = (
            sem(n) for n in ("q_evac", "q_roped", "qnT_ps", "qpT_ps", "knT_ps", "qnT_ready", "qpT_ready", "knT_ready",
                             "scores", "negmax", "probs_ready", "probsT_ps", "probsT0", "probsT1", "o_ps",
                             "gated_ready", "gT_ps", "am_hi_ready", "am_lo_ready"))
        (dT_ps, dTA_ready, dTB_ready, dscores, dnegmax, dprobs_ready, dprobsT_ps, dprobsT_ready, do_ps, do_ready,
         mdiff_ready, mexp_ready, mix_ready, bT_ps, b_hi_ready, b_lo_ready) = (
            sem(n) for n in ("dT_ps", "dTA_ready", "dTB_ready", "dscores", "dnegmax", "dprobs_ready", "dprobsT_ps",
                             "dprobsT_ready", "do_ps", "do_ready", "mdiff_ready", "mexp_ready", "mix_ready", "bT_ps",
                             "b_hi_ready", "b_lo_ready"))
        bias_loaded = [sem(f"bias_loaded{n}") for n in range(2)]
        (r_exp, merged, mT_ps, mTA_ready, mTB_ready, m_hi, m_lo, m7_hi, x_again, emb_rows, xz_ready, h_ready,
         ln_rows, ln_rows_b, shift_ready, z_out, y_done_v, y_done_p, stored) = (
            sem(n) for n in ("r_exp", "merged", "mT_ps", "mTA_ready", "mTB_ready", "m_hi", "m_lo", "m7_hi", "x_again",
                             "emb_rows", "xz_ready", "h_ready", "ln_rows", "ln_rows_b", "shift_ready", "z_out", "y_done_v", "y_done_p", "stored"))

        x_rows = x[0].rearrange("(l r) d -> r l d", r=RES)
        out_rows = out[0].rearrange("(l r) d -> r l d", r=RES)
        weights = {"in": w_in[0], "qb": w_qb[0], "kvb": w_kvb[0], "om": w_om[0], "od": w_od[0], "out": w_out[0]}
        left = {"h": (oper_hi, oper_lo), "qa": (qa_hi, qa_lo), "kva": (kva_hi, kva_lo), "am": (am_hi, am_lo),
                "b": (b_hi, b_lo)}
        block = ctx.enter_context(nc.Block())

        def tok(t):
            return slice(t * P, (t + 1) * P)

        def slot_index(section, i, n):
            return at(i, section.per_slot, section.slot0 + n)

        def chunk_index(section, i, ci):
            return at(i, section.per_chunk, section.chunk0 + ci)

        def wait_slot_done(engine, section, i, n):
            engine.wait_ge(slot_done, at(i, section.per_slot, section.slot0 + n + 1))

        def wait_before_rewrite(engine, semaphore, section, i, n):
            if i is not None or section.slot0 + n >= RING:
                engine.wait_ge(semaphore, at(i, section.per_slot, section.slot0 + n - RING + 1))

        def chunk_ahead(si, n):
            s = SECTIONS[si]
            if n < s.per_slot:
                return [c for c, ci, j, m in slots_of(s) if m == n][0]
            if si + 1 == len(SECTIONS):
                return None
            c = SECTIONS[si + 1].chunks[0]
            assert s.turns is None or (c.kt, c.width) == (s.chunks[0].kt, s.chunks[0].width)
            return c

        @block.sync
        def _(sp):
            for t in range(TT):
                for r in range(2):
                    sp.dma_start(x_sb[r * LEN:(r + 1) * LEN, t, :], x_rows[2 * t + r]).then_inc(x_loaded[t], 16)
            for s in SECTIONS:
                with turns(sp, s) as i:
                    first = [c.col if i is None else sp.snap(i * c.per + c.col) for c in s.chunks]
                    bare = [m for c, _, j, m in slots_of(s) if i is not None and j == 0 and c.col == 0]
                    for c, ci, j, n in slots_of(s):
                        if n not in bare:
                            wait_before_rewrite(sp, w_lo_ready, s, i, n + 1 if n + 1 in bare else n)
                        rows = weights[c.w][j * c.kt * P:(j + 1) * c.kt * P]
                        cols = rows[:, bass.ds(first[ci], c.width)]
                        ring = w_raw[:, n % RING, 0:c.kt * c.width].rearrange("p (a n) -> p a n", a=c.kt)
                        sp.dma_start(ring, cols.rearrange("(a p) n -> p a n", p=P)).then_inc(w_loaded[n % RING], 16)
            order = sorted([(a / len(END_VECTOR), y_done_v, a + 1, n) for a, n in enumerate(END_VECTOR)]
                           + [(a / len(END_POOL), y_done_p, a + 1, n) for a, n in enumerate(END_POOL)], key=lambda e: e[0])
            for _, done, count, n in order:
                sp.wait_ge(done, count)
                for t in range(TT):
                    for r in range(2):
                        sp.dma_start(out_rows[2 * t + r][:, n * CW:(n + 1) * CW],
                                     resid[r * LEN:(r + 1) * LEN, t, n * CW:(n + 1) * CW]).then_inc(stored, 16)
            sp.wait_ge(stored, 16 * 2 * TT * (D // CW))

        @block.tensor
        def _(pe):
            def product(s, i, c, ci, j, n):
                if j == 0 and (i is not None or s.chunk0 + ci >= 2):
                    pe.wait_ge(acc_free, at(i, s.per_chunk, s.chunk0 + ci - 1))
                pe.wait_ge(w_lo_ready, at(i, s.per_slot, s.slot0 + n + 1))
                hi, lo = left[c.left]
                result = acc[(s.chunk0 + ci) % 2]
                for a in range(c.kt):
                    k = j * c.kt + a
                    first, last = k == 0, k == c.slots * c.kt - 1
                    wh = w_hi[:, n % RING, a * c.width:(a + 1) * c.width]
                    wl = w_lo[:, n % RING, a * c.width:(a + 1) * c.width]
                    for t in range(TT):
                        y = result[:, t, 0:c.width]
                        pe.matmul(y, hi[:, k, tok(t)], wh, start=first, stop=False)
                        pe.matmul(y, hi[:, k, tok(t)], wl, start=False, stop=False)
                        ins = pe.matmul(y, lo[:, k, tok(t)], wh, start=False, stop=last)
                ins.then_inc(slot_done, 1)

            def hT_pair(b):
                pe.wait_ge(z_ready, TT * (b // 4) + TT)
                if b >= 4:
                    pe.wait_ge(hT_val, 2 * (b - 4) + 2)
                for a in range(2):
                    k = 2 * b + a
                    for t in range(TT):
                        ins = pe.transpose(BK[b % 4][:, a * SEQ + t * P:a * SEQ + (t + 1) * P],
                                           x_sb[:, t, k * P:(k + 1) * P], ident)
                ins.then_inc(hT_ps, 1)

            def before_hT(j):
                if j == 0:
                    for b in range(3):
                        hT_pair(b)
                elif j + 2 < KT // 2:
                    hT_pair(j + 2)
                pe.wait_ge(hT_lo, 2 * j + 2)

            def bias_rows():
                pe.wait_ge(bias_in, 48)
                half = (ROWLEN + 1) // 2
                for n, bank in ((0, bA), (1, bB)):
                    w = min(half, ROWLEN - n * half)
                    ins = pe.matmul(bank[0:NG * GH, 0:w], relb[:, :], bucket_sb[:, n * half:n * half + w],
                                    start=True, stop=True)
                ins.then_inc(rows_ps, 1)

            def norm_pair(src, b, event):
                bank = BK[event % 2]
                if event >= 2:
                    pe.wait_ge(nT_val, 2 * event - 2)
                for a in range(2):
                    for t in range(TT):
                        ins = pe.transpose(bank[:, a * SEQ + t * P:a * SEQ + (t + 1) * P],
                                           src[:, t, (2 * b + a) * P:(2 * b + a + 1) * P], ident)
                ins.then_inc(nT_ps, 1)

            def mla_side(step, unit1, head1, chunks):
                if step == 1:
                    pe.wait_ge(q_roped, unit1)
                    pe.wait_ge(acc_free, chunks)
                    for hh in range(2):
                        for t in range(TT):
                            ins = pe.transpose(bA[:, hh * SEQ + t * P:hh * SEQ + (t + 1) * P], q_sb[:, t, hh, 0:NOPE], ident)
                    ins.then_inc(qnT_ps, 1)
                    for hh in range(2):
                        for t in range(TT):
                            ins = pe.transpose(bC[0:ROPE, hh * SEQ + t * P:hh * SEQ + (t + 1) * P], q_sb[:, t, hh, NOPE:QHD], ident)
                    ins.then_inc(qpT_ps, 1)
                    for hh in range(2):
                        for t in range(TT):
                            ins = pe.transpose(bB[:, hh * SEQ + t * P:hh * SEQ + (t + 1) * P], k_sb[:, t, hh, :], ident)
                    ins.then_inc(knT_ps, 1)
                elif step == 2:
                    pe.wait_ge(qnT_ready, unit1)
                    pe.wait_ge(qpT_ready, unit1)
                    pe.wait_ge(knT_ready, unit1)
                    for hh, bank in ((0, bD), (1, bA)):
                        for t in range(TT):
                            y = bank[:, t * SEQ:(t + 1) * SEQ]
                            pe.matmul(y, qnT[:, hh, tok(t)], knT[:, hh, :], start=True, stop=False)
                            ins = pe.matmul(y, qpT[:, hh, tok(t)], kpeT[:, :], start=False, stop=True)
                        ins.then_inc(scores, 1)
                elif step in (4, 5):
                    hh, bank = step - 4, (bB, bC)[step - 4]
                    pe.wait_ge(probs_ready, head1 + hh)
                    for kt in range(TT):
                        for t in range(TT):
                            ins = pe.transpose(bank[:, kt * SEQ + t * P:kt * SEQ + (t + 1) * P],
                                               probs[:, hh, t, kt * P:(kt + 1) * P], ident)
                    ins.then_inc(probsT_ps, 1)
                elif step == 6:
                    for hh, ready in ((0, probsT0), (1, probsT1)):
                        pe.wait_ge(ready, unit1)
                        for t in range(TT):
                            for kt in range(TT):
                                ins = pe.matmul(bD[:, (2 * hh + t) * HD:(2 * hh + t + 1) * HD], probsT[:, hh, kt, tok(t)],
                                                v_sb[:, kt, hh, :], start=kt == 0, stop=kt == TT - 1)
                    ins.then_inc(o_ps, 1)
                elif step == 7:
                    pe.wait_ge(gated_ready, unit1)
                    for hh in range(2):
                        for t in range(TT):
                            ins = pe.transpose(bA[:, hh * SEQ + t * P:hh * SEQ + (t + 1) * P], gated[:, t, hh, :], ident)
                    ins.then_inc(gT_ps, 1)

            def heads_T(src, i, j, free):
                if j in (1, 2):
                    if j == 1:
                        pe.wait_ge(acc_free, free)
                    for hh in range(2):
                        for t in range(TT):
                            h = 2 * (j - 1) + hh
                            ins = pe.transpose(BK[j - 1][:, hh * SEQ + t * P:hh * SEQ + (t + 1) * P],
                                               src[:, t, h * HD:(h + 1) * HD], ident)
                    ins.then_inc(dT_ps, 1)

            def att(g, i, j, free):
                kw = SEQ if g == 0 else P
                head = lambda h: at(i, NG * QUAD, g * QUAD + h)
                for h in range(QUAD):
                    if j == 3 * h + 1:
                        bank = BK[h % 2]
                        if h == 0:
                            pe.wait_ge(dTA_ready, at(i, 2 * NG, 2 * g + 2))
                            pe.wait_ge(dTB_ready, at(i, 2 * NG, 2 * g + 2))
                        for t in range(TT):
                            keys = dkT[:, h, :] if g == 0 else dkT[:, h, tok(t)]
                            ins = pe.matmul(bank[:, t * kw:(t + 1) * kw], dqT[:, h, tok(t)], keys, start=True, stop=True)
                        ins.then_inc(dscores, 1)
                    if j == 3 * h + 3:
                        pe.wait_ge(dprobs_ready, head(h) + 1)
                        for t in range(TT):
                            for kt in range(kw // P):
                                ins = pe.transpose(bC[:, kt * SEQ + t * P:kt * SEQ + (t + 1) * P],
                                                   dprobs[:, t * kw + kt * P:t * kw + (kt + 1) * P], ident)
                        ins.then_inc(dprobsT_ps, 1)
                    if j == 3 * h + 4:
                        pe.wait_ge(dprobsT_ready, head(h) + 1)
                        if h == 0:
                            pe.wait_ge(acc_free, free)
                        for t in range(TT):
                            for kt in range(kw // P):
                                v = dv_sb[:, kt if g == 0 else t, h * HD:(h + 1) * HD]
                                ins = pe.matmul(bD[:, (h % 2) * SEQ + t * P:(h % 2) * SEQ + (t + 1) * P],
                                                dprobsT[:, kt * SEQ + t * P:kt * SEQ + (t + 1) * P], v,
                                                start=kt == 0, stop=kt == kw // P - 1)
                        ins.then_inc(do_ps, 1)

            def side(s, i, c, ci, j):
                if c.side == "kva0" and j == 2:
                    bias_rows()
                elif c.side == "kva1":
                    if j == 4:
                        pe.wait_ge(rows_ready, 1)
                        pe.wait_ge(rows_ready2, 1)
                        pe.wait_ge(normed, 1)
                    if j in (4, 5):
                        norm_pair(kva_sb, j - 4, j - 4)
                    if j == 6:
                        pe.wait_ge(kpe_roped, 1)
                        for t in range(TT):
                            ins = pe.transpose(bC[0:ROPE, tok(t)], kva_sb[:, t, KV_RANK:KV_RANK + ROPE], ident)
                        ins.then_inc(kpe_ps, 1)
                elif c.side == "qa1":
                    if j == 5:
                        pe.wait_ge(normed, 2)
                    if 5 <= j < 9:
                        norm_pair(qa_sb, j - 5, j - 3)
                elif c.side == "gm3" and j == 0:
                    pe.wait_ge(kpeT_ready, 1)
                elif c.side in ("mla", "mla_kv", "mla_last"):
                    step = j + 4 if c.side == "mla_kv" else j
                    unit = i if i is not None else MLA_HEADS // 2 - (1 if c.side == "mla_last" else 2)
                    mla_side(step, unit + 1, unit * 2 + 1, unit * 2 + SEC["mla"].chunk0)
                elif c.side[:2] in ("qT", "kT"):
                    if c.side[0] == "k" and j == 1:
                        pe.wait_ge(dTA_ready, at(i, 2 * NG, 2 * int(c.side[2]) + 1))
                    heads_T(a_sb, i, j, chunk_index(s, i, ci))
                elif c.side[:3] == "att":
                    att(int(c.side[3]), i, j, chunk_index(s, i, ci))
                elif c.side == "mix" and j in (8, 9):
                    if j == 8:
                        pe.wait_ge(mix_ready, at(i, 1, 1))
                    for hh in range(2):
                        for t in range(TT):
                            ins = pe.transpose(BK[j - 8][:, hh * SEQ + t * P:hh * SEQ + (t + 1) * P],
                                               o_sb[:, 0, t, 2 * (j - 8) + hh, :], ident)
                    ins.then_inc(bT_ps, 1)
                elif c.side in ("yd", "yd_last") and j in (2, 3):
                    if j == 2:
                        pe.wait_ge(merged, at(i, 1, 1 if i is not None else 8))
                    for hh in range(2):
                        for t in range(TT):
                            f = 2 * (j - 2) + hh
                            ins = pe.transpose(BK[j - 2][:, hh * SEQ + t * P:hh * SEQ + (t + 1) * P],
                                               ym[:, t, f * P:(f + 1) * P], ident)
                    ins.then_inc(mT_ps, 1)

            pe.wait_ge(consts_loaded, 96)
            pe.transpose(bD[:, 0:NV], vecs[:, :], ident[0:NV, 0:NV]).then_inc(gains_ps, 1)
            for s in SECTIONS:
                with turns(pe, s) as i:
                    for c, ci, j, n in slots_of(s):
                        if c.side == "hT":
                            if j == 1:
                                pe.wait_ge(gains_ready, 1)
                            before_hT(j)
                        if s.name == "unit0" and j == 0:
                            pe.wait_ge(nT_lo, (Q_RANK + KV_RANK) // P)
                        if c.left == "am" and j == 0:
                            pe.wait_ge(am_lo_ready, MLA_HEADS // 2)
                        if c.left == "b" and j == 0:
                            pe.wait_ge(b_lo_ready, GH // 2)
                        if s.name == "out0":
                            pe.wait_ge(m_lo, j + 1)
                        product(s, i, c, ci, j, n)
                        side(s, i, c, ci, j)

        @block.scalar
        def _(act):
            act.dma_start(vecs[0:KT, :], emb_g.rearrange("(k p) -> k p", p=P)).then_inc(consts_loaded, 16)
            act.dma_start(vecs[KT:2 * KT, :], emb_b.rearrange("(k p) -> k p", p=P)).then_inc(consts_loaded, 16)
            act.dma_start(vecs[2 * KT:2 * KT + 8, :], qa_g[0].rearrange("(k p) -> k p", p=P)).then_inc(consts_loaded, 16)
            act.dma_start(vecs[2 * KT + 8:NV, :], kva_g[0].rearrange("(k p) -> k p", p=P)).then_inc(consts_loaded, 16)
            act.dma_start(ident, ident_c).then_inc(consts_loaded, 16)
            act.dma_start(rope_sb, rope_c).then_inc(consts_loaded, 16)
            act.dma_start(relb[0:BUCKETS, :], rel_bias).then_inc(bias_in, 16)
            act.dma_start(relb[BUCKETS:BUCKETS + NG, :], group_c).then_inc(bias_in, 16)
            act.dma_start(bucket_sb[:, :], bucket_c).then_inc(bias_in, 16)

            def split_hi(s, i, c, n):
                act.wait_ge(w_loaded[n % RING], at(i, s.per_slot // RING * 16, ((s.slot0 + n) // RING + 1) * 16))
                wait_before_rewrite(act, slot_done, s, i, n)
                w = c.kt * c.width
                act.activation(w_hi[:, n % RING, 0:w], w_raw[:, n % RING, 0:w], ACT.Copy).then_inc(w_hi_ready, 1)

            def root(event):
                act.wait_ge(var_ready, event)
                act.activation(stat[:, 2:4], stat[:, 0:2], ACT.Sqrt).then_inc(sqrt_ready, 1)

            def hT_pair(b):
                act.wait_ge(hT_ps, b + 1)
                for a in range(2):
                    k = 2 * b + a
                    if k >= 4:
                        act.wait_ge(hT_lo, k - 3)
                    act.activation(h_val[:, k % 4, :], BK[b % 4][:, a * SEQ:(a + 1) * SEQ], ACT.Identity,
                                   scale=gains[:, k:k + 1], bias=gains[:, KT + k:KT + k + 1]).then_inc(hT_val, 1)

            def sums_of_squares(src, width, event):
                for t in range(TT):
                    if event or t:
                        act.wait_ge(sumsq_ready, TT * event + t)
                    act.activation(junk[:, 0:width], src[:, t, 0:width], ACT.Square,
                                   accum_out=stat[:, 4 + t:5 + t]).then_inc(sumsq_ready, 1)

            def norm_val(gain0, b, event):
                act.wait_ge(nT_ps, event + 1)
                for a in range(2):
                    k = 2 * b + a
                    if event >= 2:
                        act.wait_ge(nT_lo, 2 * event + a - 3)
                    act.activation(n_val[:, (2 * event + a) % 4, :], BK[event % 2][:, a * SEQ:(a + 1) * SEQ], ACT.Identity,
                                   scale=gains[:, gain0 + k:gain0 + k + 1]).then_inc(nT_val, 1)

            def mla_side(step, u1, h1, amd):
                if step == 1:
                    act.wait_ge(qnT_ps, u1)
                    act.activation(qnT[:, :, :].rearrange("p a b -> p (a b)"), bA[:, :], ACT.Copy).then_inc(qnT_ready, 1)
                    act.wait_ge(qpT_ps, u1)
                    act.activation(qpT[:, :, :].rearrange("p a b -> p (a b)"), bC[0:ROPE, :], ACT.Copy).then_inc(qpT_ready, 1)
                elif step == 2:
                    for hh, bank in ((0, bD), (1, bA)):
                        act.wait_ge(negmax, h1 + hh)
                        for t in range(TT):
                            c = 2 * hh + t
                            ins = act.activation(probs[:, hh, t, :], bank[:, t * SEQ:(t + 1) * SEQ], ACT.Exp,
                                                 bias=stat[:, 8 + c:9 + c], scale=MLA_SCALE, accum_out=stat[:, 12 + c:13 + c])
                        ins.then_inc(probs_ready, 1)
                elif step == 5:
                    act.wait_ge(probsT_ps, h1 + 1)
                    act.activation(probsT[:, 1, :, :].rearrange("p a b -> p (a b)"), bC[:, :], ACT.Copy).then_inc(probsT1, 1)
                elif step == 7:
                    act.wait_ge(gT_ps, u1)
                    act.activation(amd, bA[:, :].rearrange("p (a b) -> p a b", a=2), ACT.Copy).then_inc(am_hi_ready, 1)

            def att(g, i, j):
                kw = SEQ if g == 0 else P
                for h in range(QUAD):
                    n1 = at(i, NG * QUAD, g * QUAD + h + 1)
                    if j == 3 * h + 1:
                        act.wait_ge(dnegmax, n1)
                        for t in range(TT):
                            ins = act.activation(dprobs[:, t * kw:(t + 1) * kw], s_sb[:, t * kw:(t + 1) * kw], ACT.Exp,
                                                 bias=stat[:, 8 + t:9 + t],
                                                 accum_out=den_sb[:, g, t * QUAD + h:t * QUAD + h + 1])
                        ins.then_inc(dprobs_ready, 1)
                    if j == 3 * h + 3:
                        act.wait_ge(dprobsT_ps, n1)
                        w = kw // P * SEQ
                        act.activation(dprobsT[:, 0:w], bC[:, 0:w], ACT.Copy).then_inc(dprobsT_ready, 1)

            def side(s, i, c, ci, j, n):
                if c.side == "hT":
                    if j == 0:
                        for b in range(3):
                            hT_pair(b)
                    elif j + 2 < KT // 2:
                        hT_pair(j + 2)
                elif c.side == "kva0" and j == 2:
                    act.wait_ge(rows_ps, 1)
                    half = (ROWLEN + 1) // 2
                    act.activation(rowsb[:, 0:half], bA[0:NG * GH, 0:half], ACT.Copy).then_inc(rows_ready, 1)
                elif c.side == "kva1":
                    if j == 1:
                        act.wait_ge(acc_free, 2)
                        sums_of_squares(kva_sb, KV_RANK, 0)
                    if j == 2:
                        root(2)
                    if j in (4, 5):
                        norm_val(2 * KT + Q_RANK // P, j - 4, j - 4)
                    if j == 6:
                        act.wait_ge(kpe_ps, 1)
                        act.activation(kpeT[:, :], bC[0:ROPE, 0:SEQ], ACT.Copy).then_inc(kpeT_ready, 1)
                elif c.side == "qa1":
                    if j == 1:
                        act.wait_ge(acc_free, 4)
                        sums_of_squares(qa_sb, Q_RANK, 1)
                    if j == 3:
                        root(3)
                    if 5 <= j < 9:
                        norm_val(2 * KT, j - 5, j - 3)
                elif c.side[:2] == "gm" and j == 0 and c.side != "gm3_kv":
                    wait_slot_done(act, s, i, n - 1)
                    k = int(c.side[2])
                    act.activation(gm_sb[:, :, k * CW:(k + 1) * CW], acc[(s.chunk0 + ci - 1) % 2][:, :, :], ACT.Exp,
                                   scale=-1.0).then_inc(gate_exp, 1)
                elif c.side in ("mla", "mla_kv", "mla_last"):
                    step = j + 4 if c.side == "mla_kv" else j
                    unit = i if i is not None else MLA_HEADS // 2 - (1 if c.side == "mla_last" else 2)
                    heads = bass.ds(unit * 2, 2) if i is not None else slice(2 * unit, 2 * unit + 2)
                    mla_side(step, unit + 1, unit * 2 + 1, am_hi[:, heads, :])
                elif c.side[:2] in ("qT", "kT") and j == 1:
                    g = int(c.side[2])
                    e = 2 * g + (c.side[0] == "k")
                    dst = dqT if c.side[0] == "q" else dkT
                    act.wait_ge(dT_ps, at(i, 4 * NG, 2 * e + 1))
                    act.activation(dst[:, 0:2, :], bA[:, :].rearrange("p (a b) -> p a b", a=2), ACT.Copy).then_inc(dTA_ready, 1)
                elif c.side[:3] == "att":
                    att(int(c.side[3]), i, j)
                elif c.side == "mix":
                    if j == 0:
                        wait_slot_done(act, s, i, n - 1)
                        act.activation(gate_sb[:, :, :], acc[(s.chunk0 + ci - 1) % 2][:, :, :], ACT.Exp, scale=-1.0).then_inc(gate_exp, 1)
                    if j == 1:
                        act.wait_ge(mdiff_ready, at(i, 1, 1))
                        act.activation(wgt[:, :, :], wgt[:, :, :], ACT.Exp).then_inc(mexp_ready, 1)
                    if j in (8, 9):
                        act.wait_ge(bT_ps, at(i, 2, j - 7))
                        act.activation(b_hi[:, bass.ds(i * QUAD + 2 * (j - 8), 2), :], BK[j - 8][:, :].rearrange("p (a b) -> p a b", a=2),
                                       ACT.Copy).then_inc(b_hi_ready, 1)
                elif c.side in ("rm", "rd", "rd_split") and j == 0:
                    wait_slot_done(act, s, i, n - 1)
                    act.activation(sig_m if c.side == "rm" else sig_d, acc[(s.chunk0 + ci - 1) % 2][:, :, :], ACT.Exp, scale=-1.0).then_inc(r_exp, 1)
                elif c.side == "rd_split" and 1 <= j:
                    if j == 1:
                        act.wait_ge(slot_done, s.slot0 + KT // 2)
                        act.wait_ge(mTB_ready, 7)
                    for b in (2 * (j - 1), 2 * (j - 1) + 1):
                        act.activation(oper_hi[:, 2 * b:2 * b + 2, :], mT[:, 2 * b:2 * b + 2, :], ACT.Copy).then_inc(m_hi, 1)
                elif c.side == "yd" and j == 2:
                    act.wait_ge(mT_ps, at(i, 2, 1))
                    act.activation(mT[:, bass.ds(i * 4, 2), :], bA[:, :].rearrange("p (a b) -> p a b", a=2), ACT.Copy).then_inc(mTA_ready, 1)
                elif c.side == "yd_last":
                    if j in (2, 3):
                        act.wait_ge(mT_ps, 14 + j - 1)
                        k = 28 + 2 * (j - 2)
                        act.activation(oper_hi[:, k:k + 2, :], BK[j - 2][:, :].rearrange("p (a b) -> p a b", a=2), ACT.Copy).then_inc(m_hi, 1)
                    if j == 8:
                        root(4)

            act.wait_ge(gains_ps, 1)
            act.activation(gains[:, :], bD[:, 0:NV], ACT.Copy).then_inc(gains_ready, 1)
            act.wait_ge(gains_ready, 1)
            root(1)
            for n in range(AHEAD):
                split_hi(SECTIONS[0], None, chunk_ahead(0, n), n)
            for si, s in enumerate(SECTIONS):
                with turns(act, s) as i:
                    for c, ci, j, n in slots_of(s):
                        side(s, i, c, ci, j, n)
                        if chunk_ahead(si, n + AHEAD):
                            split_hi(s, i, chunk_ahead(si, n + AHEAD), n + AHEAD)
            root(5)
            act.wait_ge(shift_ready, 1)
            for n in END_POOL:
                for t in range(TT):
                    y = resid[:, t, n * CW:(n + 1) * CW]
                    ins = act.activation(y, y, ACT.Identity, scale=stat[:, 6 + t:7 + t], bias=stat[:, 8 + t:9 + t])
                ins.then_inc(z_out, 1)

        @block.vector
        def _(dve):
            steps = Steps(dve, vector_step)

            def split_lo(s, i, c, n):
                dve.wait_ge(w_hi_ready, at(i, s.per_slot, s.slot0 + n + 1))
                wait_before_rewrite(dve, slot_done, s, i, n)
                w = c.kt * c.width
                dve.tensor_tensor(w_lo[:, n % RING, 0:w], w_raw[:, n % RING, 0:w], w_hi[:, n % RING, 0:w].bitcast(F32),
                                  ALU.subtract).then_inc(w_lo_ready, 1)

            def rsqrt(event, eps):
                dve.tensor_scalar(stat[:, 0:2], stat[:, 0:2], 1.0, eps, ALU.mult, ALU.add).then_inc(var_ready, 1)
                dve.wait_ge(sqrt_ready, event)
                steps.done(dve.reciprocal(stat[:, 6:8], stat[:, 2:4]))
                steps.wait()
                steps.done(dve.tensor_tensor(stat[:, 2:4], stat[:, 6:8], stat[:, 6:8], ALU.mult))
                steps.wait()
                steps.done(dve.tensor_tensor(stat[:, 2:4], stat[:, 2:4], stat[:, 0:2], ALU.mult))
                steps.wait()
                steps.done(dve.tensor_scalar(stat[:, 2:4], stat[:, 2:4], -0.5, 1.5, ALU.mult, ALU.add))
                steps.wait()
                steps.done(dve.tensor_tensor(stat[:, 6:8], stat[:, 6:8], stat[:, 2:4], ALU.mult))
                steps.wait()

            def layer_stats(src, partials, ready):
                for t in range(TT):
                    if ready:
                        ready(t)
                    for n in range(D // CW):
                        if src is not None:
                            ins = dve.bn_stats(partials[:, t, n, :], src[:, t, n * CW:(n + 1) * CW])
                    if src is not None:
                        steps.done(ins)
                        steps.wait()
                    steps.done(dve.bn_aggr(pair[:, t, :], partials[:, t, :, :].rearrange("p a b -> p (a b)")))
                    steps.wait()
                steps.done(dve.tensor_copy(stat[:, 0:2], pair[:, :, 1]))
                steps.done(dve.tensor_copy(stat[:, 4:6], pair[:, :, 0]))
                steps.wait()

            def hT_pair(b):
                for k in (2 * b, 2 * b + 1):
                    dve.wait_ge(hT_val, k + 1)
                    dve.tensor_copy(oper_hi[:, k, :], h_val[:, k % 4, :]).then_inc(hT_hi, 1)

            def evacuate(s, i, n, pieces):
                wait_slot_done(dve, s, i, n - 1)
                for dst, src in pieces:
                    ins = dve.tensor_copy(dst, src)
                ins.then_inc(acc_free, 1)

            def scale_latent(src, width, event):
                dve.wait_ge(sumsq_ready, TT * event)
                steps.done(dve.tensor_scalar(stat[:, 0:2], stat[:, 4:6], 1.0 / width, None, ALU.mult))
                steps.wait()
                rsqrt(event + 1, RMS_EPS)
                for t in range(TT):
                    ins = dve.tensor_scalar(src[:, t, 0:width], src[:, t, 0:width], stat[:, 6 + t:7 + t], None, ALU.mult)
                ins.then_inc(normed, 1)

            def norm_split(hi, lo, b, event):
                for a in range(2):
                    k, v = 2 * b + a, n_val[:, (2 * event + a) % 4, :]
                    dve.wait_ge(nT_val, 2 * event + a + 1)
                    dve.tensor_copy(hi[:, k, :], v).then_inc(nT_hi, 1)
                    dve.wait_ge(nT_hi, 2 * event + a + 1)
                    dve.tensor_tensor(lo[:, k, :], v, hi[:, k, :].bitcast(F32), ALU.subtract).then_inc(nT_lo, 1)

            def silu(dst, src, exps):
                dve.wait_ge(gate_exp, exps)
                steps.done(dve.tensor_scalar(dst, dst, 1.0, None, ALU.add))
                steps.wait()
                steps.done(dve.reciprocal(dst, dst))
                steps.wait()
                dve.tensor_tensor(dst, dst, src, ALU.mult).then_inc(acc_free, 1)

            def mla_side(step, unit1, head1, gate, am_h, am_l):
                if step == 1:
                    dve.wait_ge(knT_ps, unit1)
                    dve.tensor_copy(knT[:, :, :].rearrange("p a b -> p (a b)"), bB[:, :]).then_inc(knT_ready, 1)
                elif step == 2:
                    for hh, bank in ((0, bD), (1, bA)):
                        dve.wait_ge(scores, head1 + hh)
                        steps.done(dve.tensor_reduce(stat[:, 8 + 2 * hh:10 + 2 * hh], bank[:, :].rearrange("p (a b) -> p a b", a=TT),
                                                     AX.X, ALU.max))
                        steps.wait()
                        dve.tensor_scalar(stat[:, 8 + 2 * hh:10 + 2 * hh], stat[:, 8 + 2 * hh:10 + 2 * hh], -MLA_SCALE, None,
                                          ALU.mult).then_inc(negmax, 1)
                elif step == 4:
                    dve.wait_ge(probsT_ps, head1)
                    dve.tensor_copy(probsT[:, 0, :, :].rearrange("p a b -> p (a b)"), bB[:, :]).then_inc(probsT0, 1)
                elif step == 6:
                    dve.wait_ge(o_ps, unit1)
                    steps.done(dve.reciprocal(stat[:, 12:16], stat[:, 12:16]))
                    steps.wait()
                    for hh in range(2):
                        for t in range(TT):
                            c = 2 * hh + t
                            ins = dve.scalar_tensor_tensor(out=gated[:, t, hh, :], in0=bD[:, c * HD:(c + 1) * HD],
                                                           scalar=stat[:, 12 + c:13 + c], in1=gate(t, hh), op0=ALU.mult, op1=ALU.mult)
                    ins.then_inc(gated_ready, 1)
                elif step == 7:
                    dve.wait_ge(am_hi_ready, unit1)
                    dve.tensor_tensor(am_l, bA[:, :].rearrange("p (a b) -> p a b", a=2), am_h.bitcast(F32),
                                      ALU.subtract).then_inc(am_lo_ready, 1)

            def evacuate_q(s, i, n):
                wait_slot_done(dve, s, i, n - 1)
                a = acc[0][:, :, 0:UNIT_Q].rearrange("p t (h d) -> p t h d", h=2)
                unit1 = at(i, 1, {"unit0": 1, "mla": 2, "mla7": 8}[s.name])
                for t in range(TT):
                    ins = dve.tensor_copy(q_sb[:, t], a[:, t])
                ins.then_inc(acc_free, 1)

            def evacuate_kv(s, i, n):
                wait_slot_done(dve, s, i, n - 1)
                a = acc[1][:, :, :].rearrange("p t (h x d) -> p t h x d", h=2, x=2)
                for t in range(TT):
                    dve.tensor_copy(k_sb[:, t], a[:, t, :, 0])
                    ins = dve.tensor_copy(v_sb[:, t], a[:, t, :, 1])
                ins.then_inc(acc_free, 1)

            def att(g, s, i, j):
                kw = SEQ if g == 0 else P
                for h in range(QUAD):
                    head = g * QUAD + h
                    n1 = at(i, NG * QUAD, head + 1)
                    if j == 3 * h + 4:
                        dve.wait_ge(do_ps, n1)
                        dve.tensor_copy(o_sb[:, g, :, h, :], bD[:, (h % 2) * SEQ:(h % 2 + 1) * SEQ].rearrange(
                            "p (t d) -> p t d", t=TT)).then_inc(do_ready, 1)
                for h in range(QUAD):
                    head = g * QUAD + h
                    n1 = at(i, NG * QUAD, head + 1)
                    if j == 3 * h + 1:
                        dve.wait_ge(dscores, n1)
                        dve.wait_ge(bias_loaded[head % 2], at(i, bias_arrivals(NG * QUAD - 2 + head % 2), bias_arrivals(head)))
                        y = s_sb[:, 0:TT * kw].rearrange("p (t k) -> p t k", t=TT)
                        if g == 0:
                            b = bias_sb[:, h % 2, :].rearrange("p (t k) -> p t k", t=TT)
                        else:
                            b = bias_sb[:, h % 2, 0:P].rearrange("p (a k) -> p a k", a=1).broadcast_to([P, TT, P])
                        steps.done(dve.scalar_tensor_tensor(
                            out=y, in0=BK[h % 2][:, 0:TT * kw].rearrange("p (t k) -> p t k", t=TT),
                            scalar=DS_SCALE, in1=b, op0=ALU.mult, op1=ALU.add))
                        steps.wait()
                        m = m_sb[:, g, :].rearrange("p (t h) -> p t h", t=TT)[:, :, h]
                        steps.done(dve.tensor_reduce(m, y, AX.X, ALU.max))
                        steps.wait()
                        dve.tensor_scalar(stat[:, 8:10], m, -1.0, None, ALU.mult).then_inc(dnegmax, 1)

            def side(s, i, c, ci, j, n):
                prev = acc[(s.chunk0 + ci - 1) % 2]
                free1 = chunk_index(s, i, ci)
                if c.side == "hT":
                    if j == 0:
                        for b in range(3):
                            hT_pair(b)
                    elif j + 2 < KT // 2:
                        hT_pair(j + 2)
                elif c.side == "kva0":
                    half = (KV_RANK + ROPE) // 2
                    if j == 0:
                        evacuate(s, i, n, [(kva_sb[:, :, 0:half], prev[:, :, 0:half])])
                    if j == 2:
                        half = (ROWLEN + 1) // 2
                        dve.wait_ge(rows_ps, 1)
                        dve.tensor_copy(rowsb[:, half:ROWLEN], bB[0:NG * GH, 0:ROWLEN - half]).then_inc(rows_ready2, 1)
                elif c.side == "kva1":
                    half = (KV_RANK + ROPE) // 2
                    if j == 0:
                        evacuate(s, i, n, [(kva_sb[:, :, half:2 * half], prev[:, :, 0:half])])
                    if j == 2:
                        scale_latent(kva_sb, KV_RANK, 1)
                    if j in (4, 5):
                        norm_split(kva_hi, kva_lo, j - 4, j - 4)
                elif c.side == "qa0" and j == 0:
                    evacuate(s, i, n, [(qa_sb[:, :, 0:CW], prev[:, :, :])])
                elif c.side == "qa1":
                    if j == 0:
                        evacuate(s, i, n, [(qa_sb[:, :, CW:2 * CW], prev[:, :, :])])
                    if j == 3:
                        scale_latent(qa_sb, Q_RANK, 2)
                    if 5 <= j < 9:
                        if j == 5:
                            dve.wait_ge(rows_stored, 16 * NG)
                        norm_split(qa_hi, qa_lo, j - 5, j - 3)
                elif c.side in ("gm0", "gm1", "gm2", "gm3") and j == 0:
                    k = int(c.side[2])
                    silu(gm_sb[:, :, k * CW:(k + 1) * CW], prev[:, :, :], k + 1)
                elif c.side == "gm3_kv" and j == 0:
                    evacuate_q(s, i, n)
                elif c.side in ("mla", "mla_kv", "mla_last"):
                    step = j + 4 if c.side == "mla_kv" else j
                    if j == 0:
                        if c.side == "mla_kv":
                            evacuate_q(s, i, n)
                        else:
                            evacuate_kv(s, i, n)
                    unit = i if i is not None else MLA_HEADS // 2 - (1 if c.side == "mla_last" else 2)
                    cols = lambda first, w: bass.ds(i * 2 * w + first, w) if i is not None \
                        else slice(unit * 2 * w + first, unit * 2 * w + first + w)
                    heads = bass.ds(i * 2, 2) if i is not None else slice(2 * unit, 2 * unit + 2)
                    mla_side(step, unit + 1, unit * 2 + 1, lambda t, hh: gm_sb[:, t, cols(hh * HD, HD)],
                             am_hi[:, heads, :], am_lo[:, heads, :])
                elif c.side[:2] in ("qT", "kT"):
                    g = int(c.side[2])
                    e = 2 * g + (c.side[0] == "k")
                    if j == 0:
                        evacuate(s, i, n, [(a_sb, prev[:, :, :])])
                    if j == 2:
                        dst = dqT if c.side[0] == "q" else dkT
                        dve.wait_ge(dT_ps, at(i, 4 * NG, 2 * e + 2))
                        dve.tensor_copy(dst[:, 2:4, :], bB[:, :].rearrange("p (a b) -> p a b", a=2)).then_inc(dTB_ready, 1)
                elif c.side[:3] == "att":
                    if j == 0:
                        evacuate(s, i, n, [(dv_sb, prev[:, :, :])])
                    att(int(c.side[3]), s, i, j)
                elif c.side == "mix":
                    merge_groups(s, i, j, prev)
                elif c.side in ("rm", "rd", "rd_split"):
                    if j == 0:
                        sig = sig_m if c.side == "rm" else sig_d
                        dve.wait_ge(r_exp, at(i, 2, (1 if c.side == "rm" else 2) + (0 if i is not None else 14)))
                        steps.done(dve.tensor_scalar(sig, sig, 1.0, None, ALU.add))
                        steps.wait()
                        dve.reciprocal(sig, sig).then_inc(acc_free, 1)
                    elif c.side == "rd_split":
                        if j == 1:
                            dve.wait_ge(slot_done, s.slot0 + KT // 2)
                        for b in (2 * (j - 1), 2 * (j - 1) + 1):
                            dve.wait_ge(m_hi, b + 1)
                            dve.tensor_tensor(oper_lo[:, 2 * b:2 * b + 2, :], mT[:, 2 * b:2 * b + 2, :],
                                              oper_hi[:, 2 * b:2 * b + 2, :].bitcast(F32), ALU.subtract).then_inc(m_lo, 1)
                elif c.side == "ym" and j == 0:
                    wait_slot_done(dve, s, i, n - 1)
                    dve.wait_ge(acc_free, at(i, s.per_chunk, s.chunk0 + ci - 1))
                    dve.tensor_tensor(ym, prev[:, :, :], sig_m, ALU.mult).then_inc(acc_free, 1)
                elif c.side in ("yd", "yd_last"):
                    if j == 0:
                        wait_slot_done(dve, s, i, n - 1)
                        dve.tensor_tensor(sig_d, prev[:, :, :], sig_d, ALU.mult).then_inc(acc_free, 1)
                        dve.wait_ge(acc_free, free1)
                        dve.tensor_tensor(ym, ym, sig_d, ALU.add).then_inc(merged, 1)
                    if c.side == "yd" and j == 3:
                        dve.wait_ge(mT_ps, at(i, 2, 2))
                        dve.tensor_copy(mT[:, bass.ds(i * 4 + 2, 2), :], bB[:, :].rearrange("p (a b) -> p a b", a=2)).then_inc(mTB_ready, 1)
                    if c.side == "yd_last" and j in (2, 3):
                        k = 28 + 2 * (j - 2)
                        dve.wait_ge(m_hi, 13 + j)
                        dve.tensor_tensor(oper_lo[:, k:k + 2, :], BK[j - 2][:, :].rearrange("p (a b) -> p a b", a=2),
                                          oper_hi[:, k:k + 2, :].bitcast(F32), ALU.subtract).then_inc(m_lo, 1)
                    if c.side == "yd_last" and j in (6, 7):
                        t = j - 6
                        dve.wait_ge(x_again, 64)
                        for m in range(D // CW):
                            ins = dve.bn_stats(xbn[:, t, m, :], resid[:, t, m * CW:(m + 1) * CW])
                        steps.done(ins)
                    if c.side == "yd_last" and j == 8:
                        steps.wait()
                        layer_stats(None, xbn, None)
                        rsqrt(4, LN_EPS)
                    if c.side == "yd_last" and j in (9, 10):
                        t = j - 9
                        dve.tensor_scalar(resid[:, t, :], resid[:, t, :], stat[:, 4 + t:5 + t], stat[:, 6 + t:7 + t],
                                          ALU.subtract, ALU.mult).then_inc(xz_ready, 1)
                elif c.side[:3] == "fin" and j == 0:
                    residual(s, i, n, int(c.side[3]), prev)

            def residual(s, i, n, block0, prev):
                wait_slot_done(dve, s, i, n - 1)
                blocks = SEC["out"].per_chunk
                dve.wait_ge(h_ready, at(i, blocks, block0 + 1))
                cols = bass.ds(i * (blocks * CW) + block0 * CW, CW) if i is not None else slice(block0 * CW, (block0 + 1) * CW)
                y = resid[:, :, cols]
                dve.scalar_tensor_tensor(out=y, in0=y, scalar=ALPHA, in1=prev[:, :, :], op0=ALU.mult,
                                         op1=ALU.add).then_inc(acc_free, 1)
                dve.wait_ge(acc_free, at(i, blocks, SEC["out0"].chunk0 + block0 + 1))
                part = bass.ds(i * blocks + block0, 1) if i is not None else slice(block0, block0 + 1)
                for t in range(TT):
                    ins = dve.bn_stats(ybn[:, t, part, :].rearrange("p a b -> p (a b)"), resid[:, t, cols])
                steps.done(ins)

            def merge_groups(s, i, j, prev):
                if j == 0:
                    silu(gate_sb[:, :, :], prev[:, :, :], at(i, 1, 5))
                    steps.done(dve.tensor_tensor(big_m, m_sb[:, 0], m_sb[:, 1], ALU.max))
                    steps.wait()
                    steps.done(dve.tensor_tensor(big_m, big_m, m_sb[:, 2], ALU.max))
                    steps.wait()
                    for g in range(NG):
                        ins = dve.tensor_tensor(wgt[:, g], m_sb[:, g], big_m, ALU.subtract)
                    ins.then_inc(mdiff_ready, 1)
                elif j == 1:
                    dve.wait_ge(mexp_ready, at(i, 1, 1))
                    steps.done(dve.tensor_tensor(den_sb, den_sb, wgt, ALU.mult))
                    steps.wait()
                    steps.done(dve.tensor_tensor(big_m, den_sb[:, 0], den_sb[:, 1], ALU.add))
                    steps.wait()
                    steps.done(dve.tensor_tensor(big_m, big_m, den_sb[:, 2], ALU.add))
                    steps.wait()
                    steps.done(dve.reciprocal(big_m, big_m))
                    steps.wait()
                    for g in range(NG):
                        ins = dve.tensor_tensor(wgt[:, g], wgt[:, g], big_m, ALU.mult)
                    steps.done(ins)
                    steps.wait()
                elif j in (2, 3, 4):
                    g = j - 2
                    o = o_sb[:, g].rearrange("p t h d -> p (t h) d")
                    w = wgt[:, g].rearrange("p (a b) -> p a b", b=1).broadcast_to([P, TT * QUAD, HD])
                    steps.done(dve.tensor_tensor(o, o, w, ALU.mult))
                    steps.wait()
                elif j in (5, 6):
                    g = j - 4
                    steps.done(dve.tensor_tensor(o_sb[:, 0], o_sb[:, 0], o_sb[:, g], ALU.add))
                    steps.wait()
                elif j == 7:
                    dve.tensor_tensor(o_sb[:, 0], o_sb[:, 0], gate_sb.rearrange("p t (h d) -> p t h d", h=QUAD),
                                      ALU.mult).then_inc(mix_ready, 1)
                elif j in (8, 9):
                    dve.wait_ge(b_hi_ready, at(i, 2, j - 7))
                    heads = bass.ds(i * QUAD + 2 * (j - 8), 2)
                    dve.tensor_tensor(b_lo[:, heads, :], BK[j - 8][:, :].rearrange("p (a b) -> p a b", a=2),
                                      b_hi[:, heads, :].bitcast(F32), ALU.subtract).then_inc(b_lo_ready, 1)

            layer_stats(x_sb, bn, lambda t: dve.wait_ge(x_loaded[t], 32))
            rsqrt(1, LN_EPS)
            W = D // 4
            for n in range(4):
                for t in range(TT):
                    dve.tensor_scalar(x_sb[:, t, n * W:(n + 1) * W], x_sb[:, t, n * W:(n + 1) * W], stat[:, 4 + t:5 + t],
                                      stat[:, 6 + t:7 + t], ALU.subtract, ALU.mult).then_inc(z_ready, 1)
            for n in range(AHEAD):
                split_lo(SECTIONS[0], None, chunk_ahead(0, n), n)
            for si, s in enumerate(SECTIONS):
                with turns(dve, s) as i:
                    steps.enter(i, VECTOR_STEPS.get(s.name, 0))
                    for c, ci, j, n in slots_of(s):
                        side(s, i, c, ci, j, n)
                        if chunk_ahead(si, n + AHEAD):
                            split_lo(s, i, chunk_ahead(si, n + AHEAD), n + AHEAD)
                    steps.leave(s.turns)
            last = D // CW - 1
            residual(SECTIONS[-1], None, KT // 2, last, acc[1])
            steps.wait()
            layer_stats(None, ybn, None)
            rsqrt(5, LN_EPS)
            steps.done(dve.tensor_tensor(stat[:, 8:10], stat[:, 4:6], stat[:, 6:8], ALU.mult))
            steps.wait()
            dve.tensor_scalar(stat[:, 8:10], stat[:, 8:10], -1.0, None, ALU.mult).then_inc(shift_ready, 1)
            dve.wait_ge(ln_rows, 16)
            dve.wait_ge(ln_rows_b, 16)
            for n in END_VECTOR:
                cols = slice(n * CW, (n + 1) * CW)
                for t in range(TT):
                    steps.done(dve.scalar_tensor_tensor(out=resid[:, t, cols], in0=resid[:, t, cols], scalar=stat[:, 4 + t:5 + t],
                                                        in1=ln_g_row[:, cols], op0=ALU.subtract, op1=ALU.mult))
                steps.wait()
                for t in range(TT):
                    ins = dve.scalar_tensor_tensor(out=resid[:, t, cols], in0=resid[:, t, cols], scalar=stat[:, 6 + t:7 + t],
                                                   in1=ln_b_row[:, cols], op0=ALU.mult, op1=ALU.add)
                ins.then_inc(y_done_v, 1)

        @block.gpsimd
        def _(pool):
            steps = Steps(pool, pool_step)

            def rotate(v, tmp, done, shape):
                half = ROPE // 2
                if shape is None:
                    cos, sin = rope_sb[:, 0], rope_sb[:, 1]
                    a, b = (slice(None),) * 2 + (slice(0, half),), (slice(None),) * 2 + (slice(half, ROPE),)
                else:
                    cos, sin = (rope_sb[:, n].rearrange("p t (a d) -> p t a d", a=1).broadcast_to(shape) for n in range(2))
                    a, b = (slice(None),) * 3 + (slice(0, half),), (slice(None),) * 3 + (slice(half, ROPE),)
                pool.tensor_tensor(tmp[a], v[b], sin[a], ALU.mult)
                steps.done(pool.tensor_tensor(tmp[b], v[a], sin[b], ALU.mult))
                steps.wait()
                steps.done(pool.tensor_tensor(v, v, cos, ALU.mult))
                steps.wait()
                pool.tensor_tensor(v, v, tmp, ALU.add).then_inc(done, 1)

            def load_bias(quad, head):
                g, h = head // QUAD, head % QUAD
                b = head % 2
                first = (g * GH + quad * QUAD + h) * LEN * PITCH
                n_before = quad * NG * QUAD + head
                if n_before >= 2:
                    pool.wait_ge(dnegmax, n_before - 1)
                for t in range(TT if g == 0 else 1):
                    n = RES if g == 0 else 2
                    for r in range(2):
                        dst = bias_sb[r * LEN:(r + 1) * LEN, b, t * SEQ:t * SEQ + n * LEN].rearrange("p (r k) -> p r k", r=n)
                        off = (RES - 1 - r - 2 * t) * NDL + LEN - 1
                        src = bass.AP(tensor=bias_rows_d.tensor, offset=first + off, ap=[[PITCH - 1, LEN], [NDL, n], [1, LEN]])
                        pool.dma_start(dst, src).then_inc(bias_loaded[b], 16)

            for k in range(KT):
                pool.wait_ge(hT_hi, k + 1)
                pool.tensor_tensor(oper_lo[:, k, :], h_val[:, k % 4, :], oper_hi[:, k, :].bitcast(F32),
                                   ALU.subtract).then_inc(hT_lo, 1)
            pool.wait_ge(rows_ready, 1)
            pool.wait_ge(rows_ready2, 1)
            for g in range(NG):
                src = rowsb[g * GH:(g + 1) * GH, 0:ROWLEN].rearrange("p (a n) -> p a n", a=1).broadcast_to([GH, LEN, ROWLEN])
                pool.dma_start(bias_rows_d[g * GH:(g + 1) * GH, :, 0:ROWLEN], src).then_inc(rows_stored, 16)
            pool.wait_ge(normed, 1)
            rotate(kva_sb[:, :, KV_RANK:KV_RANK + ROPE], ropet, kpe_roped, None)
            pool.wait_ge(rows_stored, 16 * NG)
            shape = [P, TT, 2, ROPE]
            for n, (turns_, chunks0) in enumerate(((None, SEC["unit0"].chunk0 + 1), (6, SEC["mla"].chunk0 + 1), (None, SEC["mla7"].chunk0 + 1))):
                def one(i):
                    pool.wait_ge(acc_free, at(i, 2, chunks0))
                    rotate(q_sb[:, :, :, NOPE:QHD], qrope, q_roped, shape)
                if turns_ is None:
                    one(None)
                else:
                    with pool.Fori(0, turns_) as i:
                        steps.enter(i, POOL_STEPS["mla"])
                        one(i)
                    steps.leave(turns_)
            pool.wait_ge(am_lo_ready, MLA_HEADS // 2)
            for quad in range(GH // QUAD):
                for head in range(NG * QUAD):
                    load_bias(quad, head)

            merge7 = SEC["merge7"]
            pool.wait_ge(slot_done, merge7.slot0 + merge7.chunks[0].slots + merge7.chunks[1].slots)
            for t in range(TT):
                for r in range(2):
                    pool.dma_start(resid[r * LEN:(r + 1) * LEN, t, :], x_rows[2 * t + r]).then_inc(x_again, 16)
            pool.wait_ge(slot_done, merge7.slot0 + merge7.per_slot)
            pool.dma_start(ln_g_row, ln_g[0:1, :].broadcast_to([P, D])).then_inc(ln_rows, 16)
            pool.wait_ge(m_lo, KT // 2 - 2)
            pool.dma_start(emb_g_row, emb_g.rearrange("(a n) -> a n", a=1).broadcast_to([P, D])).then_inc(emb_rows, 16)
            pool.dma_start(emb_b_row, emb_b.rearrange("(a n) -> a n", a=1).broadcast_to([P, D])).then_inc(emb_rows, 16)
            pool.wait_ge(emb_rows, 32)
            pool.wait_ge(xz_ready, TT)
            for n in range(D // CW):
                cols = slice(n * CW, (n + 1) * CW)
                for t in range(TT):
                    steps.done(pool.tensor_tensor(resid[:, t, cols], resid[:, t, cols], emb_g_row[:, cols], ALU.mult))
                steps.wait()
                for t in range(TT):
                    ins = pool.tensor_tensor(resid[:, t, cols], resid[:, t, cols], emb_b_row[:, cols], ALU.add)
                ins.then_inc(h_ready, 1)
            pool.wait_ge(h_ready, D // CW)
            pool.dma_start(ln_b_row, ln_b[0:1, :].broadcast_to([P, D])).then_inc(ln_rows_b, 16)
            pool.wait_ge(ln_rows, 16)
            pool.wait_ge(ln_rows_b, 16)
            for a, n in enumerate(END_POOL):
                cols = slice(n * CW, (n + 1) * CW)
                pool.wait_ge(z_out, a + 1)
                for t in range(TT):
                    steps.done(pool.tensor_tensor(resid[:, t, cols], resid[:, t, cols], ln_g_row[:, cols], ALU.mult))
                steps.wait()
                for t in range(TT):
                    ins = pool.tensor_tensor(resid[:, t, cols], resid[:, t, cols], ln_b_row[:, cols], ALU.add)
                ins.then_inc(y_done_p, 1)


def kernel(x, emb_ln_g, emb_ln_b, rel_bias, w_in, q_a_norm_g, w_q_b, kv_a_norm_g, w_kv_b, w_o_mla, w_o_dswa, w_out,
           ln_g, ln_b):
    import concourse.bacc as bacc
    from concourse.bass_utils import run_bass_kernel_spmd as run

    nc = bacc.Bacc("TRN2", target_bir_lowering=False, num_devices=1)
    given = {"x": x, "emb_ln_g": emb_ln_g, "emb_ln_b": emb_ln_b, "rel_bias": rel_bias, "w_in": w_in,
             "q_a_norm_g": q_a_norm_g, "w_q_b": w_q_b, "kv_a_norm_g": kv_a_norm_g, "w_kv_b": w_kv_b,
             "w_o_mla": w_o_mla, "w_o_dswa": w_o_dswa, "w_out": w_out, "ln_g": ln_g, "ln_b": ln_b}
    arrays, args = {}, []
    for name, value in given.items():
        a = np.ascontiguousarray(value)
        arrays[f"in_{name}"] = a
        args.append(nc.dram_tensor(f"in_{name}", a.shape, mybir.dt.from_np(a.dtype), kind="ExternalInput").ap())
    out = nc.dram_tensor("out_h", (1, SEQ, D), F32, kind="ExternalOutput").ap()
    program(nc, *args, out)
    return run(nc, [arrays], core_ids=[0]).results[0]["out_h"]
```

```python
import numpy as np
from contextlib import ExitStack, contextmanager
import concourse.bass as bass
from concourse import mybir

F32 = mybir.dt.float32
F32R = mybir.dt.float32r
ALU = mybir.AluOpType
ACT = mybir.ActivationFunctionType
AX = mybir.AxisListType

P = 128
D = 4096
SEQ = 256
TT = SEQ // P
Q_RANK, KV_RANK = 1024, 512
MLA_HEADS, NOPE, ROPE, HD = 16, 128, 64, 128
QHD = NOPE + ROPE
MLA_W = MLA_HEADS * HD
GROUPS = ((128, 1), (512, 4), (2048, 16))
NG, GH = len(GROUPS), 8
DS_W = GH * HD
QKV_W = NG * DS_W
BUCKETS, MAX_DIST = 32, 1024
ALPHA = 2.0 ** 0.25
LN_EPS, RMS_EPS, NEG = 1e-5, 1e-6, -1e30
MLA_SCALE, DS_SCALE = QHD ** -0.5, HD ** -0.5
COL_QA = 0
COL_KVA = COL_QA + Q_RANK
COL_DQ = COL_KVA + KV_RANK + ROPE
COL_DK = COL_DQ + QKV_W
COL_DV = COL_DK + QKV_W
COL_GM = COL_DV + QKV_W
COL_GD = COL_GM + MLA_W
COL_RM = COL_GD + DS_W
COL_RD = COL_RM + D

RES, LEN = 4, SEQ // 4
NDR, NDL = 2 * RES - 1, 2 * LEN - 1
ROWLEN = NDR * NDL
PITCH = 896

CW = 512
RING = 4
XPARTS = 4
AHEAD = 3
KT = D // P
QUAD = CW // HD
UNIT_Q = 2 * QHD


def positions():
    t, p = np.meshgrid(np.arange(TT), np.arange(P), indexing="ij")
    return 4 * (p % LEN) + 2 * t + p // LEN


def rope_table():
    inv = np.float32(1.0) / (np.float32(10000.0) ** (np.arange(0, ROPE, 2, dtype=np.float32) / np.float32(ROPE)))
    ang = (positions().astype(np.float32)[:, :, None] * inv[None, None, :].astype(np.float32)).astype(np.float32)
    cos, sin = np.cos(ang.astype(np.float64)), np.sin(ang.astype(np.float64))
    both = np.stack([np.concatenate([cos, cos], -1), np.concatenate([-sin, sin], -1)], 0)
    return np.ascontiguousarray(both.transpose(2, 0, 1, 3).astype(np.float32))


def bucket_table():
    dr, dl = np.meshgrid(np.arange(NDR) - (RES - 1), np.arange(NDL) - (LEN - 1), indexing="ij")
    rel = (RES * dl + dr).reshape(-1)
    nb = BUCKETS // 2
    exact = nb // 2
    n = np.abs(rel)
    large = exact + (np.log(np.maximum(n, 1) / exact) / np.log(MAX_DIST / exact) * (nb - exact)).astype(np.int64)
    b = np.where(rel > 0, nb, 0) + np.where(n < exact, n, np.minimum(large, nb - 1))
    table = np.zeros((BUCKETS + NG, rel.size), np.float32)
    table[b, np.arange(rel.size)] = 1.0
    for g, (window, dil) in enumerate(GROUPS):
        ok = (n % dil == 0) & (n <= window // 2)
        table[BUCKETS + g] = np.where(ok, 0.0, NEG)
    return table


class Chunk:

    def __init__(self, w, col, per, left, slots, kt, width, side):
        self.w, self.col, self.per, self.left = w, col, per, left
        self.slots, self.kt, self.width, self.side = slots, kt, width, side


class Section:

    def __init__(self, name, turns, chunks):
        self.name, self.turns, self.chunks = name, turns, chunks
        self.per_slot, self.per_chunk = sum(c.slots for c in chunks), len(chunks)


def sections():
    def full(col, per, side, w="in"):
        return Chunk(w, col, per, "h", KT // 2, 2, CW, side)

    def unit(u, per, side):
        return [Chunk("qb", UNIT_Q * u, per * UNIT_Q, "qa", 4, 2, UNIT_Q, side),
                Chunk("kvb", CW * u, per * CW, "kva", 4, 1, CW, side + "_kv")]

    half = (KV_RANK + ROPE) // 2
    body = []
    for g in range(NG):
        c = g * DS_W
        if g:
            body.append(full(COL_DQ + c, CW, f"att{g - 1}"))
        body.append(full(COL_DK + c, CW, f"qT{g}"))
        body.append(full(COL_DV + c, CW, f"kT{g}"))
    body.append(full(COL_GD, CW, f"att{NG - 1}"))
    body.append(full(COL_DQ + CW, COL_RM - (COL_DQ + CW), "mix"))
    out = [
        Section("start", None,
                [full(COL_QA, 0, "hT")]
                + [Chunk("in", COL_KVA + half * n, 0, "h", KT // 2, 2, half, s) for n, s in ((0, "qa0"), (1, "kva0"))]
                + [full(COL_QA + CW, 0, "kva1"), full(COL_GM, 0, "qa1")]
                + [full(COL_GM + CW * n, 0, f"gm{n - 1}") for n in (1, 2, 3)]),
        Section("unit0", None, unit(0, 0, "gm3")),
        Section("mla", 6, unit(1, 1, "mla")),
        Section("mla7", None, unit(7, 0, "mla")),
        Section("dq0", None, [full(COL_DQ, 0, "mla_last")]),
        Section("dswa", 2, body),
        Section("merge", 7, [
            full(COL_RD, CW, "rm"),
            Chunk("om", 0, CW, "am", 8, 2, CW, "rd"),
            Chunk("od", 0, CW, "b", 4, 2, CW, "ym"),
            full(COL_RM + CW, CW, "yd")]),
        Section("merge7", None, [
            full(COL_RD + 7 * CW, 0, "rm"),
            Chunk("om", 7 * CW, 0, "am", 8, 2, CW, "rd_split"),
            Chunk("od", 7 * CW, 0, "b", 4, 2, CW, "ym")]),
        Section("out0", None, [full(0, 0, "yd_last", "out")]),
        Section("out", 3, [full(CW, 2 * CW, "fin0", "out"), full(2 * CW, 2 * CW, "fin1", "out")]),
        Section("out7", None, [full(7 * CW, 0, "fin6", "out")]),
    ]
    slot = chunk = 0
    for s in out:
        s.slot0, s.chunk0 = slot, chunk
        slot += s.per_slot * (s.turns or 1)
        chunk += s.per_chunk * (s.turns or 1)
        assert s.slot0 % RING == 0 and s.per_slot % RING == 0
        assert s.turns is None or s.per_chunk % 2 == 0
    return out


SECTIONS = sections()
SEC = {s.name: s for s in SECTIONS}


def at(i, per, base):
    return base if i is None else i * per + base


@contextmanager
def turns(nc, engine, section):
    if section.turns is None:
        yield None
    else:
        with nc.Fori(0, section.turns, engines=(engine.engine,), hint_back_edge=True) as i:
            yield i


def slots_of(section):
    n = 0
    for ci, c in enumerate(section.chunks):
        for j in range(c.slots):
            yield c, ci, j, n
            n += 1


class Steps:

    def __init__(self, engine, sem):
        self.engine, self.sem, self.n, self.i, self.per = engine, sem, 0, None, 0

    def enter(self, i, per):
        self.i, self.per, self.base = i, per, self.n

    def leave(self, turns_):
        if self.i is not None:
            assert self.n - self.base == self.per, (self.sem, self.n - self.base)
            self.n = self.base + self.per * turns_
            self.i = None

    def done(self, ins):
        ins.then_inc(self.sem, 1)
        self.n += 1

    def wait(self):
        self.engine.wait_ge(self.sem, at(self.i, self.per, self.n))


VECTOR_STEPS = {"mla": 3, "dswa": 36, "out": 2}
POOL_STEPS = {"mla": 2}


def pieces(*cuts):
    return [slice(a * D // 32, b * D // 32) for a, b in zip(cuts, cuts[1:])]


END_VECTOR, END_POOL = pieces(0, 4, 8, 12, 16, 20, 21), pieces(21, 28, 32)
STORES = (("v", 0), ("v", 1), ("v", 2), ("v", 3), ("p", 0), ("v", 4), ("v", 5), ("p", 1))


def bias_dmas(head):
    return 2 * TT if head < QUAD else 2


def bias_arrivals(head):
    return 16 * sum(bias_dmas(n) for n in range(head + 1) if n % 2 == head % 2)


def program(nc, x, emb_g, emb_b, rel_bias, w_in, qa_g, w_qb, kva_g, w_kvb, w_om, w_od, w_out, ln_g, ln_b, out):
    ident_c = nc.inline_tensor(np.eye(P, dtype=np.float32), name="identity_const").ap()
    rope_c = nc.inline_tensor(rope_table(), name="rope_const").ap()
    bucket_c = nc.inline_tensor(bucket_table(), name="bucket_const").ap()
    group_c = nc.inline_tensor(np.repeat(np.eye(NG, dtype=np.float32), GH, axis=1), name="group_const").ap()
    h_kept = nc.dram_tensor("h_kept", (D // CW, P, TT, CW), F32).ap()
    bias_rows_d = nc.dram_tensor("bias_rows", (NG * GH, LEN, PITCH), F32).ap()

    with ExitStack() as ctx:
        K = 1024
        base = (nc.sbuf_base + 31) // 32 * 32
        OPER = base
        RINGS = OPER + 64 * K
        R_A = RINGS + 48 * K
        R_B = R_A + 32 * K
        R_C = R_B + 16 * K
        SMALL = R_C + 32 * K

        def sb(name, at_, shape, dt=F32):
            return nc.alloc_sbuf_tensor_at(name, shape, dt, offset=at_).ap()

        oper_hi = sb("oper_hi", OPER, [P, KT, SEQ], F32R)
        oper_lo = sb("oper_lo", OPER + 32 * K, [P, KT, SEQ], F32R)
        w_raw = sb("w_raw", RINGS, [P, RING, 2 * CW])
        w_hi = sb("w_hi", RINGS + 16 * K, [P, RING, 2 * CW], F32R)
        w_lo = sb("w_lo", RINGS + 32 * K, [P, RING, 2 * CW], F32R)
        x_sb = sb("x_sb", R_A, [P, TT, D])
        am_hi = sb("am_hi", R_A, [P, MLA_HEADS, SEQ], F32R)
        am_lo = sb("am_lo", R_A + 16 * K, [P, MLA_HEADS, SEQ], F32R)
        resid = sb("resid", R_A, [P, TT, D])
        bucket_sb = sb("bucket_sb", R_B, [BUCKETS + NG, ROWLEN])
        rowsb = sb("rowsb", R_B + 4 * K, [NG * GH, PITCH])
        relb = sb("relb", R_B + 8 * K, [BUCKETS + NG, NG * GH])
        qa_hi = sb("qa_hi", R_B, [P, Q_RANK // P, SEQ], F32R)
        qa_lo = sb("qa_lo", R_B + 8 * K, [P, Q_RANK // P, SEQ], F32R)
        b_hi = sb("b_hi", R_B, [P, GH, SEQ], F32R)
        b_lo = sb("b_lo", R_B + 8 * K, [P, GH, SEQ], F32R)
        ln_g_row = sb("ln_g_row", R_B, [P, D])
        h_val = sb("h_val", R_C, [P, 4, SEQ])
        emb_rows = [sb(f"emb_rows{n}", R_C + (4 + 8 * n) * K, [P, 2, CW]) for n in range(2)]
        gm_sb = sb("gm_sb", R_C, [P, TT, MLA_W])
        kva_hi = sb("kva_hi", R_C + 16 * K, [P, KV_RANK // P, SEQ], F32R)
        kva_lo = sb("kva_lo", R_C + 20 * K, [P, KV_RANK // P, SEQ], F32R)
        qa_sb = sb("qa_sb", R_C + 24 * K, [P, TT, Q_RANK])
        q_sb = sb("q_sb", R_C + 24 * K, [P, TT, 2, QHD])
        v_sb = sb("v_sb", R_C + 27 * K, [P, TT, 2, HD])
        qn_hi = sb("qn_hi", R_C + 29 * K, [P, 2, SEQ], F32R)
        a_sb = sb("a_sb", R_C, [P, TT, CW])
        dv_sb = sb("dv_sb", R_C + 4 * K, [P, TT, CW])
        dqT = sb("dqT", R_C + 8 * K, [P, QUAD, SEQ])
        dkT = sb("dkT", R_C + 12 * K, [P, QUAD, SEQ])
        o_sb = sb("o_sb", R_C + 16 * K, [P, NG, TT, QUAD, HD])
        gate_sb = sb("gate_sb", R_C + 28 * K, [P, TT, CW])
        mT = sb("mT", R_C, [P, KT, SEQ])
        ln_b_row = sb("ln_b_row", R_C, [P, D])
        o = SMALL
        ident = sb("ident", o, [P, P])
        rope_sb = sb("rope_sb", o + 512, [P, 2, TT, ROPE])
        kpeT = sb("kpeT", o + 1536, [P, SEQ], F32R)
        NV = 2 * KT + Q_RANK // P + KV_RANK // P
        gains = sb("gains", o + 2560, [P, NV])
        stat = sb("stat", o + 2880, [P, 16])
        pair = sb("pair", o + 3264, [P, TT, 2])
        m_sb = sb("m_sb", o + 2944, [P, NG, TT * QUAD])
        den_sb = sb("den_sb", o + 3040, [P, NG, TT * QUAD])
        big_m = sb("big_m", o + 3136, [P, TT * QUAD])
        wgt = sb("wgt", o + 3168, [P, NG, TT * QUAD])
        TAIL = o + 3296
        vecs = sb("vecs", TAIL, [NV, P])
        bn = sb("bn", TAIL + 512, [P, TT, D // CW, 6])
        kva_sb = sb("kva_sb", TAIL + 1024, [P, TT, KV_RANK + ROPE])
        ropet = sb("ropet", TAIL + 6 * K, [P, TT, ROPE])
        junk = sb("junk", TAIL + 7 * K, [P, Q_RANK])
        n_val = sb("n_val", TAIL + 7 * K, [P, 4, SEQ])
        kn_hi = sb("kn_hi", TAIL, [P, 2, SEQ], F32R)
        gated = sb("gated", TAIL, [P, TT, 2, HD])
        qp_hi = sb("qp_hi", TAIL + 2 * K, [P, 2, SEQ], F32R)
        qp_lo = sb("qp_lo", TAIL + 6 * K, [ROPE, 2, SEQ], F32R)
        qn_lo = sb("qn_lo", TAIL + 8 * K, [P, 2, SEQ], F32R)
        kn_lo = sb("kn_lo", TAIL + 10 * K, [P, 2, SEQ], F32R)
        probs = sb("probs", TAIL + 4 * K, [P, 2, TT, SEQ])
        k_sb = sb("k_sb", TAIL + 4 * K, [P, TT, 2, HD])
        probsT = sb("probsT", TAIL + 8 * K, [P, 2, TT, SEQ])
        qrope = sb("qrope", R_C + 31 * K, [P, TT, 2, ROPE])
        bias_sb = sb("bias_sb", TAIL, [P, 2, TT * SEQ])
        s_sb = sb("s_sb", TAIL + 4 * K, [P, TT * SEQ])
        dprobs = sb("dprobs", TAIL + 6 * K, [P, TT * SEQ])
        dprobsT = sb("dprobsT", TAIL + 8 * K, [P, TT * SEQ])
        sig_m = sb("sig_m", TAIL, [P, TT, CW])
        sig_d = sb("sig_d", TAIL + 4 * K, [P, TT, CW])
        ym = sb("ym", TAIL + 8 * K, [P, TT, CW])
        ybn = sb("ybn", TAIL + 512, [P, TT, D // CW, 6])
        assert TAIL + 12 * K <= nc.sbuf_usable_end, (TAIL + 12 * K, nc.sbuf_usable_end)

        acc = [ctx.enter_context(nc.psum_tensor(f"acc{n}", [P, TT, CW], F32)) for n in range(2)]
        BK = [ctx.enter_context(nc.psum_tensor(f"bank{n}", [P, CW], F32)) for n in range(4)]
        bA, bB, bC, bD = BK

        def sem(name):
            return ctx.enter_context(nc.semaphore(name))

        w_loaded = [sem(f"w_loaded{n}") for n in range(RING)]
        w_hi_ready, w_lo_ready, slot_done, acc_free = (sem(n) for n in ("w_hi_ready", "w_lo_ready", "slot_done", "acc_free"))
        x_loaded = [sem(f"x_loaded{n}") for n in range(XPARTS)]
        consts_loaded, bias_in = sem("consts_loaded"), sem("bias_in")
        vector_step, pool_step, sqrt_ready, var_ready = (sem(n) for n in ("vector_step", "pool_step", "sqrt_ready", "var_ready"))
        gains_ps, gains_ready = sem("gains_ps"), sem("gains_ready")
        z_ready, hT_ps, hT_hi, hT_val, hT_lo = (sem(n) for n in ("z_ready", "hT_ps", "hT_hi", "hT_val", "hT_lo"))
        rows_ps, rows_ready, rows_ready2, rows_stored = (sem(n) for n in ("rows_ps", "rows_ready", "rows_ready2", "rows_stored"))
        sumsq_ready, normed, nT_ps, nT_hi, nT_val, nT_lo = (sem(n) for n in ("sumsq_ready", "normed", "nT_ps", "nT_hi", "nT_val", "nT_lo"))
        kpe_roped, kpe_ps, kpe_hi_ready, kpe_lo_ready = (sem(n) for n in ("kpe_roped", "kpe_ps", "kpe_hi_ready", "kpe_lo_ready"))
        gate_sig = sem("gate_sig")
        (q_roped, qnT_ps, qpT_ps, knT_ps, qn_hi_ready, qp_hi_ready, kn_hi_ready, qk_lo_ready, scores, negmax, probs_ready,
         probsT_ps, probsT0, probsT1, o_ps, gated_ready, gT_ps, am_hi_ready, am_lo_ready) = (
            sem(n) for n in ("q_roped", "qnT_ps", "qpT_ps", "knT_ps", "qn_hi_ready", "qp_hi_ready", "kn_hi_ready",
                             "qk_lo_ready", "scores", "negmax", "probs_ready", "probsT_ps", "probsT0", "probsT1", "o_ps",
                             "gated_ready", "gT_ps", "am_hi_ready", "am_lo_ready"))
        (dT_ps, dTA_ready, dTB_ready, dscores, dnegmax, dprobs_ready, dprobsT_ps, dprobsT_ready, do_ps, do_ready,
         mdiff_ready, mexp_ready, mix_ready, bT_ps, b_hi_ready, b_lo_ready) = (
            sem(n) for n in ("dT_ps", "dTA_ready", "dTB_ready", "dscores", "dnegmax", "dprobs_ready", "dprobsT_ps",
                             "dprobsT_ready", "do_ps", "do_ready", "mdiff_ready", "mexp_ready", "mix_ready", "bT_ps",
                             "b_hi_ready", "b_lo_ready"))
        bias_loaded = [sem(f"bias_loaded{n}") for n in range(2)]
        (r_sig, merged, mT_ps, mTA_ready, mTB_ready, m_hi, m_lo, h_done, h_stored, ln_rows, ln_rows_b, shift_ready,
         z_out, y_done_v, y_done_p, stored) = (
            sem(n) for n in ("r_sig", "merged", "mT_ps", "mTA_ready", "mTB_ready", "m_hi", "m_lo", "h_done", "h_stored",
                             "ln_rows", "ln_rows_b", "shift_ready", "z_out", "y_done_v", "y_done_p", "stored"))
        emb_loaded, h_again = ([sem(f"{name}{n}") for n in range(2)] for name in ("emb_loaded", "h_again"))

        x_rows = x[0].rearrange("(l t r) d -> r l t d", t=TT, r=2)
        out_rows = out[0].rearrange("(l t r) d -> r l t d", t=TT, r=2)
        weights = {"in": w_in[0], "qb": w_qb[0], "kvb": w_kvb[0], "om": w_om[0], "od": w_od[0], "out": w_out[0]}
        left = {"h": (oper_hi, oper_lo), "qa": (qa_hi, qa_lo), "kva": (kva_hi, kva_lo), "am": (am_hi, am_lo),
                "b": (b_hi, b_lo)}
        block = ctx.enter_context(nc.Block())

        def tok(t):
            return slice(t * P, (t + 1) * P)

        def chunk_index(section, i, ci):
            return at(i, section.per_chunk, section.chunk0 + ci)

        def wait_slot_done(engine, section, i, n):
            engine.wait_ge(slot_done, at(i, section.per_slot, section.slot0 + n + 1))

        def wait_before_rewrite(engine, semaphore, section, i, n):
            if i is not None or section.slot0 + n >= RING:
                engine.wait_ge(semaphore, at(i, section.per_slot, section.slot0 + n - RING + 1))

        def chunk_ahead(si, n):
            s = SECTIONS[si]
            if n < s.per_slot:
                return [c for c, ci, j, m in slots_of(s) if m == n][0]
            if si + 1 == len(SECTIONS):
                return None
            c = SECTIONS[si + 1].chunks[0]
            assert s.turns is None or (c.kt, c.width) == (s.chunks[0].kt, s.chunks[0].width)
            return c

        @block.sync
        def _(sp):
            for n in range(XPARTS):
                cols = slice(n * D // XPARTS, (n + 1) * D // XPARTS)
                for r in range(2):
                    sp.dma_start(x_sb[r * LEN:(r + 1) * LEN, :, cols], x_rows[r][:, :, cols]).then_inc(x_loaded[n], 16)
            for s in SECTIONS:
                with turns(nc, sp, s) as i:
                    first = [c.col if i is None else sp.snap(i * c.per + c.col) for c in s.chunks]
                    bare = [m for c, _, j, m in slots_of(s) if i is not None and j == 0 and c.col == 0]
                    for c, ci, j, n in slots_of(s):
                        if n not in bare:
                            wait_before_rewrite(sp, w_lo_ready, s, i, n + 1 if n + 1 in bare else n)
                        rows = weights[c.w][j * c.kt * P:(j + 1) * c.kt * P]
                        cols = rows[:, bass.ds(first[ci], c.width)]
                        ring = w_raw[:, n % RING, 0:c.kt * c.width].rearrange("p (a n) -> p a n", a=c.kt)
                        sp.dma_start(ring, cols.rearrange("(a p) n -> p a n", p=P)).then_inc(w_loaded[n % RING], 16)
            for who, n in STORES:
                cols, done = (END_VECTOR[n], y_done_v) if who == "v" else (END_POOL[n], y_done_p)
                sp.wait_ge(done, n + 1)
                for r in range(2):
                    sp.dma_start(out_rows[r][:, :, cols], resid[r * LEN:(r + 1) * LEN, :, cols]).then_inc(stored, 16)
            sp.wait_ge(stored, 16 * 2 * len(STORES))

        @block.tensor
        def _(pe):
            def product(s, i, c, ci, j, n):
                if j == 0 and (i is not None or s.chunk0 + ci >= 2):
                    pe.wait_ge(acc_free, at(i, s.per_chunk, s.chunk0 + ci - 1))
                pe.wait_ge(w_lo_ready, at(i, s.per_slot, s.slot0 + n + 1))
                hi, lo = left[c.left]
                result = acc[(s.chunk0 + ci) % 2]
                for a in range(c.kt):
                    k = j * c.kt + a
                    first, last = k == 0, k == c.slots * c.kt - 1
                    wh = w_hi[:, n % RING, a * c.width:(a + 1) * c.width]
                    wl = w_lo[:, n % RING, a * c.width:(a + 1) * c.width]
                    for t in range(TT):
                        y = result[:, t, 0:c.width]
                        pe.matmul(y, hi[:, k, tok(t)], wh, start=first, stop=False)
                        pe.matmul(y, hi[:, k, tok(t)], wl, start=False, stop=False)
                        ins = pe.matmul(y, lo[:, k, tok(t)], wh, start=False, stop=last)
                ins.then_inc(slot_done, 1)

            def hT_pair(b):
                pe.wait_ge(z_ready, TT * (b // 4) + TT)
                if b >= 4:
                    pe.wait_ge(hT_val, 2 * (b - 4) + 2)
                for a in range(2):
                    k = 2 * b + a
                    for t in range(TT):
                        ins = pe.transpose(BK[b % 4][:, a * SEQ + t * P:a * SEQ + (t + 1) * P],
                                           x_sb[:, t, k * P:(k + 1) * P], ident)
                ins.then_inc(hT_ps, 1)

            def before_hT(j):
                if j == 0:
                    for b in range(3):
                        hT_pair(b)
                elif j + 2 < KT // 2:
                    hT_pair(j + 2)
                pe.wait_ge(hT_lo, 2 * j + 2)

            def bias_rows():
                pe.wait_ge(bias_in, 64)
                half = (ROWLEN + 1) // 2
                for n, bank in ((0, bA), (1, bB)):
                    w = min(half, ROWLEN - n * half)
                    ins = pe.matmul(bank[0:NG * GH, 0:w], relb[:, :], bucket_sb[:, n * half:n * half + w],
                                    start=True, stop=True)
                ins.then_inc(rows_ps, 1)

            def norm_pair(src, b, event):
                bank = BK[event % 2]
                if event >= 2:
                    pe.wait_ge(nT_val, 2 * event - 2)
                for a in range(2):
                    for t in range(TT):
                        ins = pe.transpose(bank[:, a * SEQ + t * P:a * SEQ + (t + 1) * P],
                                           src[:, t, (2 * b + a) * P:(2 * b + a + 1) * P], ident)
                ins.then_inc(nT_ps, 1)

            def mla_side(step, unit1, head1, chunks):
                if step == 1:
                    pe.wait_ge(q_roped, unit1)
                    pe.wait_ge(acc_free, chunks)
                    for hh in range(2):
                        for t in range(TT):
                            ins = pe.transpose(bA[:, hh * SEQ + t * P:hh * SEQ + (t + 1) * P], q_sb[:, t, hh, 0:NOPE], ident)
                    ins.then_inc(qnT_ps, 1)
                    for hh in range(2):
                        for t in range(TT):
                            ins = pe.transpose(bC[0:ROPE, hh * SEQ + t * P:hh * SEQ + (t + 1) * P], q_sb[:, t, hh, NOPE:QHD], ident)
                    ins.then_inc(qpT_ps, 1)
                    for hh in range(2):
                        for t in range(TT):
                            ins = pe.transpose(bB[:, hh * SEQ + t * P:hh * SEQ + (t + 1) * P], k_sb[:, t, hh, :], ident)
                    ins.then_inc(knT_ps, 1)
                elif step == 3:
                    pe.wait_ge(qk_lo_ready, unit1)
                    for hh, bank in ((0, bD), (1, bA)):
                        for t in range(TT):
                            y = bank[:, t * SEQ:(t + 1) * SEQ]
                            pe.matmul(y, qn_hi[:, hh, tok(t)], kn_hi[:, hh, :], start=True, stop=False)
                            pe.matmul(y, qn_hi[:, hh, tok(t)], kn_lo[:, hh, :], start=False, stop=False)
                            pe.matmul(y, qn_lo[:, hh, tok(t)], kn_hi[:, hh, :], start=False, stop=False)
                            pe.matmul(y, qp_hi[:, hh, tok(t)], kpeT[:, :], start=False, stop=False)
                            ins = pe.matmul(y, qp_lo[:, hh, tok(t)], kpeT[0:ROPE, :], start=False, stop=True)
                        ins.then_inc(scores, 1)
                elif step == 5:
                    for hh, bank in ((0, bB), (1, bC)):
                        pe.wait_ge(probs_ready, head1 + hh)
                        for kt in range(TT):
                            for t in range(TT):
                                ins = pe.transpose(bank[:, kt * SEQ + t * P:kt * SEQ + (t + 1) * P],
                                                   probs[:, hh, t, kt * P:(kt + 1) * P], ident)
                        ins.then_inc(probsT_ps, 1)
                elif step == 6:
                    for hh, ready in ((0, probsT0), (1, probsT1)):
                        pe.wait_ge(ready, unit1)
                        for t in range(TT):
                            for kt in range(TT):
                                ins = pe.matmul(bD[:, (2 * hh + t) * HD:(2 * hh + t + 1) * HD], probsT[:, hh, kt, tok(t)],
                                                v_sb[:, kt, hh, :], start=kt == 0, stop=kt == TT - 1)
                    ins.then_inc(o_ps, 1)
                elif step == 7:
                    pe.wait_ge(gated_ready, unit1)
                    for hh in range(2):
                        for t in range(TT):
                            ins = pe.transpose(bA[:, hh * SEQ + t * P:hh * SEQ + (t + 1) * P], gated[:, t, hh, :], ident)
                    ins.then_inc(gT_ps, 1)

            def heads_T(src, i, j, free):
                if j in (1, 2):
                    if j == 1:
                        pe.wait_ge(acc_free, free)
                    for hh in range(2):
                        for t in range(TT):
                            h = 2 * (j - 1) + hh
                            ins = pe.transpose(BK[j - 1][:, hh * SEQ + t * P:hh * SEQ + (t + 1) * P],
                                               src[:, t, h * HD:(h + 1) * HD], ident)
                    ins.then_inc(dT_ps, 1)

            def att(g, i, j, free):
                kw = SEQ if g == 0 else P
                head = lambda h: at(i, NG * QUAD, g * QUAD + h)
                for h in range(QUAD):
                    if j == 3 * h + 1:
                        bank = BK[h % 2]
                        if h == 0:
                            pe.wait_ge(dTA_ready, at(i, 2 * NG, 2 * g + 2))
                            pe.wait_ge(dTB_ready, at(i, 2 * NG, 2 * g + 2))
                        for t in range(TT):
                            keys = dkT[:, h, :] if g == 0 else dkT[:, h, tok(t)]
                            ins = pe.matmul(bank[:, t * kw:(t + 1) * kw], dqT[:, h, tok(t)], keys, start=True, stop=True)
                        ins.then_inc(dscores, 1)
                    if j == 3 * h + 3:
                        pe.wait_ge(dprobs_ready, head(h) + 1)
                        for t in range(TT):
                            for kt in range(kw // P):
                                ins = pe.transpose(bC[:, kt * SEQ + t * P:kt * SEQ + (t + 1) * P],
                                                   dprobs[:, t * kw + kt * P:t * kw + (kt + 1) * P], ident)
                        ins.then_inc(dprobsT_ps, 1)
                    if j == 3 * h + 4:
                        pe.wait_ge(dprobsT_ready, head(h) + 1)
                        if h == 0:
                            pe.wait_ge(acc_free, free)
                        for t in range(TT):
                            for kt in range(kw // P):
                                v = dv_sb[:, kt if g == 0 else t, h * HD:(h + 1) * HD]
                                ins = pe.matmul(bD[:, (h % 2) * SEQ + t * P:(h % 2) * SEQ + (t + 1) * P],
                                                dprobsT[:, kt * SEQ + t * P:kt * SEQ + (t + 1) * P], v,
                                                start=kt == 0, stop=kt == kw // P - 1)
                        ins.then_inc(do_ps, 1)

            def side(s, i, c, ci, j):
                if c.side == "qa0" and j == 2:
                    bias_rows()
                elif c.side == "kva1":
                    if j == 6:
                        pe.wait_ge(rows_ready, 1)
                        pe.wait_ge(rows_ready2, 1)
                        pe.wait_ge(normed, 1)
                    if j in (6, 7):
                        norm_pair(kva_sb, j - 6, j - 6)
                    if j == 8:
                        pe.wait_ge(kpe_roped, 1)
                        for t in range(TT):
                            ins = pe.transpose(bC[0:ROPE, tok(t)], kva_sb[:, t, KV_RANK:KV_RANK + ROPE], ident)
                        ins.then_inc(kpe_ps, 1)
                elif c.side == "qa1":
                    if j == 6:
                        pe.wait_ge(normed, 2)
                    if 6 <= j < 10:
                        norm_pair(qa_sb, j - 6, j - 4)
                elif c.side == "gm3" and j == 0:
                    pe.wait_ge(kpe_lo_ready, 1)
                elif c.side in ("mla", "mla_kv", "mla_last"):
                    step = j + 4 if c.side == "mla_kv" else j
                    unit = i if i is not None else MLA_HEADS // 2 - (1 if c.side == "mla_last" else 2)
                    mla_side(step, unit + 1, unit * 2 + 1, unit * 2 + SEC["mla"].chunk0)
                elif c.side[:2] in ("qT", "kT"):
                    if c.side[0] == "k" and j == 1:
                        pe.wait_ge(dTA_ready, at(i, 2 * NG, 2 * int(c.side[2]) + 1))
                    heads_T(a_sb, i, j, chunk_index(s, i, ci))
                elif c.side[:3] == "att":
                    att(int(c.side[3]), i, j, chunk_index(s, i, ci))
                elif c.side == "mix" and j in (8, 9):
                    if j == 8:
                        pe.wait_ge(mix_ready, at(i, 1, 1))
                    for hh in range(2):
                        for t in range(TT):
                            ins = pe.transpose(BK[j - 8][:, hh * SEQ + t * P:hh * SEQ + (t + 1) * P],
                                               o_sb[:, 0, t, 2 * (j - 8) + hh, :], ident)
                    ins.then_inc(bT_ps, 1)
                elif c.side in ("yd", "yd_last") and j in (2, 3):
                    if j == 2:
                        pe.wait_ge(merged, at(i, 1, 1 if i is not None else 8))
                    for hh in range(2):
                        for t in range(TT):
                            f = 2 * (j - 2) + hh
                            ins = pe.transpose(BK[j - 2][:, hh * SEQ + t * P:hh * SEQ + (t + 1) * P],
                                               ym[:, t, f * P:(f + 1) * P], ident)
                    ins.then_inc(mT_ps, 1)

            pe.wait_ge(consts_loaded, 80)
            pe.transpose(bD[:, 0:NV], vecs[:, :], ident[0:NV, 0:NV]).then_inc(gains_ps, 1)
            for s in SECTIONS:
                with turns(nc, pe, s) as i:
                    for c, ci, j, n in slots_of(s):
                        if c.side == "hT":
                            if j == 1:
                                pe.wait_ge(gains_ready, 1)
                            before_hT(j)
                        if s.name == "unit0" and j == 0:
                            pe.wait_ge(nT_lo, (Q_RANK + KV_RANK) // P)
                        if c.left == "am" and j == 0:
                            pe.wait_ge(am_lo_ready, MLA_HEADS // 2)
                        if c.left == "b" and j == 0:
                            pe.wait_ge(b_lo_ready, GH // 2)
                        if s.name == "out0":
                            pe.wait_ge(m_lo, j + 1)
                        product(s, i, c, ci, j, n)
                        side(s, i, c, ci, j)

        @block.scalar
        def _(act):
            act.dma_start(vecs[0:KT, :], emb_g.rearrange("(k p) -> k p", p=P)).then_inc(consts_loaded, 16)
            act.dma_start(vecs[KT:2 * KT, :], emb_b.rearrange("(k p) -> k p", p=P)).then_inc(consts_loaded, 16)
            act.dma_start(vecs[2 * KT:2 * KT + 8, :], qa_g[0].rearrange("(k p) -> k p", p=P)).then_inc(consts_loaded, 16)
            act.dma_start(vecs[2 * KT + 8:NV, :], kva_g[0].rearrange("(k p) -> k p", p=P)).then_inc(consts_loaded, 16)
            act.dma_start(ident, ident_c).then_inc(consts_loaded, 16)
            act.dma_start(rope_sb, rope_c).then_inc(bias_in, 16)
            act.dma_start(relb[0:BUCKETS, :], rel_bias).then_inc(bias_in, 16)
            act.dma_start(relb[BUCKETS:BUCKETS + NG, :], group_c).then_inc(bias_in, 16)
            act.dma_start(bucket_sb[:, :], bucket_c).then_inc(bias_in, 16)

            def split_hi(s, i, c, n):
                act.wait_ge(w_loaded[n % RING], at(i, s.per_slot // RING * 16, ((s.slot0 + n) // RING + 1) * 16))
                wait_before_rewrite(act, slot_done, s, i, n)
                w = c.kt * c.width
                act.activation(w_hi[:, n % RING, 0:w], w_raw[:, n % RING, 0:w], ACT.Copy).then_inc(w_hi_ready, 1)

            def root(event):
                act.wait_ge(var_ready, event)
                act.activation(stat[:, 2:4], stat[:, 0:2], ACT.Sqrt).then_inc(sqrt_ready, 1)

            def hT_pair(b):
                act.wait_ge(hT_ps, b + 1)
                for a in range(2):
                    k = 2 * b + a
                    if k >= 4:
                        act.wait_ge(hT_lo, k - 3)
                    act.activation(h_val[:, k % 4, :], BK[b % 4][:, a * SEQ:(a + 1) * SEQ], ACT.Identity,
                                   scale=gains[:, k:k + 1], bias=gains[:, KT + k:KT + k + 1]).then_inc(hT_val, 1)

            def sums_of_squares(src, width, event):
                for t in range(TT):
                    if event or t:
                        act.wait_ge(sumsq_ready, TT * event + t)
                    act.activation(junk[:, 0:width], src[:, t, 0:width], ACT.Square,
                                   accum_out=stat[:, 4 + t:5 + t]).then_inc(sumsq_ready, 1)

            def norm_val(gain0, b, event):
                act.wait_ge(nT_ps, event + 1)
                for a in range(2):
                    k = 2 * b + a
                    if event >= 2:
                        act.wait_ge(nT_lo, 2 * event + a - 3)
                    act.activation(n_val[:, (2 * event + a) % 4, :], BK[event % 2][:, a * SEQ:(a + 1) * SEQ], ACT.Identity,
                                   scale=gains[:, gain0 + k:gain0 + k + 1]).then_inc(nT_val, 1)

            def mla_side(step, u1, h1, amd):
                if step == 1:
                    act.wait_ge(qnT_ps, u1)
                    act.activation(qn_hi[:, :, :].rearrange("p a b -> p (a b)"), bA[:, :], ACT.Copy).then_inc(qn_hi_ready, 1)
                    act.wait_ge(qpT_ps, u1)
                    for half in range(2):
                        ins = act.activation(qp_hi[half * ROPE:(half + 1) * ROPE, :, :].rearrange("p a b -> p (a b)"),
                                             bC[0:ROPE, :], ACT.Copy)
                    ins.then_inc(qp_hi_ready, 1)
                    act.wait_ge(knT_ps, u1)
                    act.activation(kn_hi[:, :, :].rearrange("p a b -> p (a b)"), bB[:, :], ACT.Copy).then_inc(kn_hi_ready, 1)
                elif step == 3:
                    for hh, bank in ((0, bD), (1, bA)):
                        act.wait_ge(negmax, h1 + hh)
                        for t in range(TT):
                            c = 2 * hh + t
                            ins = act.activation(probs[:, hh, t, :], bank[:, t * SEQ:(t + 1) * SEQ], ACT.Exp,
                                                 bias=stat[:, 8 + c:9 + c], scale=MLA_SCALE, accum_out=stat[:, 12 + c:13 + c])
                        ins.then_inc(probs_ready, 1)
                elif step == 5:
                    act.wait_ge(probsT_ps, h1 + 1)
                    act.activation(probsT[:, 1, :, :].rearrange("p a b -> p (a b)"), bC[:, :], ACT.Copy).then_inc(probsT1, 1)
                elif step == 7:
                    act.wait_ge(gT_ps, u1)
                    act.activation(amd, bA[:, :].rearrange("p (a b) -> p a b", a=2), ACT.Copy).then_inc(am_hi_ready, 1)

            def att(g, i, j):
                kw = SEQ if g == 0 else P
                for h in range(QUAD):
                    n1 = at(i, NG * QUAD, g * QUAD + h + 1)
                    if j == 3 * h + 1:
                        act.wait_ge(dnegmax, n1)
                        for t in range(TT):
                            ins = act.activation(dprobs[:, t * kw:(t + 1) * kw], s_sb[:, t * kw:(t + 1) * kw], ACT.Exp,
                                                 bias=stat[:, 8 + t:9 + t],
                                                 accum_out=den_sb[:, g, t * QUAD + h:t * QUAD + h + 1])
                        ins.then_inc(dprobs_ready, 1)
                    if j == 3 * h + 3:
                        act.wait_ge(dprobsT_ps, n1)
                        w = kw // P * SEQ
                        act.activation(dprobsT[:, 0:w], bC[:, 0:w], ACT.Copy).then_inc(dprobsT_ready, 1)

            def side(s, i, c, ci, j, n):
                if c.side == "hT":
                    if 0 < j and j + 2 < KT // 2:
                        hT_pair(j + 2)
                elif c.side == "qa0" and j == 2:
                    act.wait_ge(rows_ps, 1)
                    half = (ROWLEN + 1) // 2
                    act.activation(rowsb[:, 0:half], bA[0:NG * GH, 0:half], ACT.Copy).then_inc(rows_ready, 1)
                elif c.side == "kva1":
                    if j == 1:
                        act.wait_ge(acc_free, 3)
                        sums_of_squares(kva_sb, KV_RANK, 0)
                    if j == 3:
                        root(2)
                    if j in (6, 7):
                        norm_val(2 * KT + Q_RANK // P, j - 6, j - 6)
                    if j == 8:
                        act.wait_ge(kpe_ps, 1)
                        act.activation(kpeT[0:ROPE, :], bC[0:ROPE, 0:SEQ], ACT.Copy).then_inc(kpe_hi_ready, 1)
                elif c.side == "qa1":
                    if j == 1:
                        act.wait_ge(acc_free, 4)
                        sums_of_squares(qa_sb, Q_RANK, 1)
                    if j == 3:
                        root(3)
                    if 6 <= j < 10:
                        norm_val(2 * KT, j - 6, j - 4)
                elif c.side[:2] == "gm" and j == 0 and c.side != "gm3_kv":
                    wait_slot_done(act, s, i, n - 1)
                    k = int(c.side[2])
                    if k == 2:
                        act.wait_ge(h_stored, 16 * (D // CW))
                    act.activation(gm_sb[:, :, k * CW:(k + 1) * CW], acc[(s.chunk0 + ci - 1) % 2][:, :, :],
                                   ACT.Sigmoid).then_inc(gate_sig, 1)
                elif c.side in ("mla", "mla_kv", "mla_last"):
                    step = j + 4 if c.side == "mla_kv" else j
                    unit = i if i is not None else MLA_HEADS // 2 - (1 if c.side == "mla_last" else 2)
                    heads = bass.ds(unit * 2, 2) if i is not None else slice(2 * unit, 2 * unit + 2)
                    mla_side(step, unit + 1, unit * 2 + 1, am_hi[:, heads, :])
                elif c.side[:2] in ("qT", "kT") and j == 1:
                    g = int(c.side[2])
                    e = 2 * g + (c.side[0] == "k")
                    dst = dqT if c.side[0] == "q" else dkT
                    act.wait_ge(dT_ps, at(i, 4 * NG, 2 * e + 1))
                    act.activation(dst[:, 0:2, :], bA[:, :].rearrange("p (a b) -> p a b", a=2), ACT.Copy).then_inc(dTA_ready, 1)
                elif c.side[:3] == "att":
                    att(int(c.side[3]), i, j)
                elif c.side == "mix":
                    if j == 0:
                        wait_slot_done(act, s, i, n - 1)
                        act.activation(gate_sb[:, :, :], acc[(s.chunk0 + ci - 1) % 2][:, :, :], ACT.Sigmoid).then_inc(gate_sig, 1)
                    if j == 1:
                        act.wait_ge(mdiff_ready, at(i, 1, 1))
                        act.activation(wgt[:, :, :], wgt[:, :, :], ACT.Exp).then_inc(mexp_ready, 1)
                    if j in (8, 9):
                        act.wait_ge(bT_ps, at(i, 2, j - 7))
                        act.activation(b_hi[:, bass.ds(i * QUAD + 2 * (j - 8), 2), :], BK[j - 8][:, :].rearrange("p (a b) -> p a b", a=2),
                                       ACT.Copy).then_inc(b_hi_ready, 1)
                elif c.side in ("rm", "rd", "rd_split") and j == 0:
                    wait_slot_done(act, s, i, n - 1)
                    act.activation(sig_m if c.side == "rm" else sig_d, acc[(s.chunk0 + ci - 1) % 2][:, :, :],
                                   ACT.Sigmoid).then_inc(r_sig, 1)
                elif c.side == "rd_split" and 1 <= j:
                    if j == 1:
                        act.wait_ge(slot_done, s.slot0 + KT // 2)
                        act.wait_ge(mTB_ready, 7)
                    for b in (2 * (j - 1), 2 * (j - 1) + 1):
                        act.activation(oper_hi[:, 2 * b:2 * b + 2, :], mT[:, 2 * b:2 * b + 2, :], ACT.Copy).then_inc(m_hi, 1)
                elif c.side == "yd" and j == 2:
                    act.wait_ge(mT_ps, at(i, 2, 1))
                    act.activation(mT[:, bass.ds(i * 4, 2), :], bA[:, :].rearrange("p (a b) -> p a b", a=2), ACT.Copy).then_inc(mTA_ready, 1)
                elif c.side == "yd_last":
                    if j in (2, 3):
                        act.wait_ge(mT_ps, 14 + j - 1)
                        k = 28 + 2 * (j - 2)
                        act.activation(oper_hi[:, k:k + 2, :], BK[j - 2][:, :].rearrange("p (a b) -> p a b", a=2), ACT.Copy).then_inc(m_hi, 1)

            act.wait_ge(gains_ps, 1)
            act.activation(gains[:, :], bD[:, 0:NV], ACT.Copy).then_inc(gains_ready, 1)
            act.wait_ge(gains_ready, 1)
            act.activation(stat[:, 14:15], ident[:, 0:1], ACT.Sqrt)
            root(1)
            for n in range(AHEAD):
                split_hi(SECTIONS[0], None, chunk_ahead(0, n), n)
            for b in range(AHEAD):
                hT_pair(b)
            for si, s in enumerate(SECTIONS):
                with turns(nc, act, s) as i:
                    for c, ci, j, n in slots_of(s):
                        side(s, i, c, ci, j, n)
                        if chunk_ahead(si, n + AHEAD):
                            split_hi(s, i, chunk_ahead(si, n + AHEAD), n + AHEAD)
            root(4)
            act.wait_ge(shift_ready, 1)
            for cols in END_POOL:
                for t in range(TT):
                    y = resid[:, t, cols]
                    ins = act.activation(y, y, ACT.Identity, scale=stat[:, 6 + t:7 + t], bias=stat[:, 8 + t:9 + t])
                ins.then_inc(z_out, 1)

        @block.vector
        def _(dve):
            steps = Steps(dve, vector_step)

            def split_lo(s, i, c, n):
                dve.wait_ge(w_hi_ready, at(i, s.per_slot, s.slot0 + n + 1))
                wait_before_rewrite(dve, slot_done, s, i, n)
                w = c.kt * c.width
                dve.tensor_tensor(w_lo[:, n % RING, 0:w], w_raw[:, n % RING, 0:w], w_hi[:, n % RING, 0:w].bitcast(F32),
                                  ALU.subtract).then_inc(w_lo_ready, 1)

            def after_root(event):
                dve.wait_ge(sqrt_ready, event)
                steps.done(dve.reciprocal(stat[:, 6:8], stat[:, 2:4]))
                steps.wait()
                steps.done(dve.tensor_tensor(stat[:, 2:4], stat[:, 6:8], stat[:, 6:8], ALU.mult))
                steps.wait()
                steps.done(dve.tensor_tensor(stat[:, 2:4], stat[:, 2:4], stat[:, 0:2], ALU.mult))
                steps.wait()
                steps.done(dve.tensor_scalar(stat[:, 2:4], stat[:, 2:4], -0.5, 1.5, ALU.mult, ALU.add))
                steps.wait()
                steps.done(dve.tensor_tensor(stat[:, 6:8], stat[:, 6:8], stat[:, 2:4], ALU.mult))
                steps.wait()

            def aggregate(partials):
                for t in range(TT):
                    ins = dve.bn_aggr(pair[:, t, :], partials[:, t, :, :].rearrange("p a b -> p (a b)"))
                steps.done(ins)
                steps.wait()
                dve.tensor_copy(stat[:, 4:6], pair[:, :, 0])
                dve.tensor_scalar(stat[:, 0:2], pair[:, :, 1], 1.0, LN_EPS, ALU.mult, ALU.add).then_inc(var_ready, 1)

            def hT_pair(b):
                for k in (2 * b, 2 * b + 1):
                    dve.wait_ge(hT_val, k + 1)
                    dve.tensor_copy(oper_hi[:, k, :], h_val[:, k % 4, :]).then_inc(hT_hi, 1)

            def evacuate(s, i, n, pieces):
                wait_slot_done(dve, s, i, n - 1)
                for dst, src in pieces:
                    ins = dve.tensor_copy(dst, src)
                ins.then_inc(acc_free, 1)

            def scale_latent(src, width, event, part):
                if part == 0:
                    dve.wait_ge(sumsq_ready, TT * event)
                    dve.tensor_scalar(stat[:, 0:2], stat[:, 4:6], 1.0 / width, RMS_EPS, ALU.mult, ALU.add).then_inc(var_ready, 1)
                elif part == 1:
                    after_root(event + 1)
                else:
                    for t in range(TT):
                        ins = dve.tensor_scalar(src[:, t, 0:width], src[:, t, 0:width], stat[:, 6 + t:7 + t], None, ALU.mult)
                    ins.then_inc(normed, 1)

            def norm_split(hi, lo, b, event):
                for a in range(2):
                    k, v = 2 * b + a, n_val[:, (2 * event + a) % 4, :]
                    dve.wait_ge(nT_val, 2 * event + a + 1)
                    dve.tensor_copy(hi[:, k, :], v).then_inc(nT_hi, 1)
                    dve.wait_ge(nT_hi, 2 * event + a + 1)
                    dve.tensor_tensor(lo[:, k, :], v, hi[:, k, :].bitcast(F32), ALU.subtract).then_inc(nT_lo, 1)

            def silu(dst, src, sigmoids):
                dve.wait_ge(gate_sig, sigmoids)
                dve.tensor_tensor(dst, dst, src, ALU.mult).then_inc(acc_free, 1)

            def mla_side(step, unit1, head1, gate, am_h, am_l):
                if step == 1:
                    for ready, hi, lo, bank in ((qn_hi_ready, qn_hi, qn_lo, bA), (qp_hi_ready, qp_hi[0:ROPE], qp_lo, bC[0:ROPE]),
                                                (kn_hi_ready, kn_hi, kn_lo, bB)):
                        dve.wait_ge(ready, unit1)
                        ins = dve.tensor_tensor(lo, bank.rearrange("p (a b) -> p a b", a=2), hi.bitcast(F32), ALU.subtract)
                    ins.then_inc(qk_lo_ready, 1)
                elif step == 3:
                    for hh, bank in ((0, bD), (1, bA)):
                        dve.wait_ge(scores, head1 + hh)
                        steps.done(dve.tensor_reduce(stat[:, 8 + 2 * hh:10 + 2 * hh], bank[:, :].rearrange("p (a b) -> p a b", a=TT),
                                                     AX.X, ALU.max))
                        steps.wait()
                        dve.tensor_scalar(stat[:, 8 + 2 * hh:10 + 2 * hh], stat[:, 8 + 2 * hh:10 + 2 * hh], -MLA_SCALE, None,
                                          ALU.mult).then_inc(negmax, 1)
                elif step == 5:
                    dve.wait_ge(probsT_ps, head1)
                    dve.tensor_copy(probsT[:, 0, :, :].rearrange("p a b -> p (a b)"), bB[:, :]).then_inc(probsT0, 1)
                    dve.wait_ge(probs_ready, head1 + 1)
                    steps.done(dve.reciprocal(stat[:, 12:16], stat[:, 12:16]))
                elif step == 6:
                    steps.wait()
                    dve.wait_ge(o_ps, unit1)
                    for hh in range(2):
                        for t in range(TT):
                            c = 2 * hh + t
                            ins = dve.scalar_tensor_tensor(out=gated[:, t, hh, :], in0=bD[:, c * HD:(c + 1) * HD],
                                                           scalar=stat[:, 12 + c:13 + c], in1=gate(t, hh), op0=ALU.mult, op1=ALU.mult)
                    ins.then_inc(gated_ready, 1)
                elif step == 7:
                    dve.wait_ge(am_hi_ready, unit1)
                    dve.tensor_tensor(am_l, bA[:, :].rearrange("p (a b) -> p a b", a=2), am_h.bitcast(F32),
                                      ALU.subtract).then_inc(am_lo_ready, 1)

            def evacuate_q(s, i, n):
                wait_slot_done(dve, s, i, n - 1)
                a = acc[0][:, :, 0:UNIT_Q].rearrange("p t (h d) -> p t h d", h=2)
                for t in range(TT):
                    ins = dve.tensor_copy(q_sb[:, t], a[:, t])
                ins.then_inc(acc_free, 1)

            def evacuate_kv(s, i, n):
                wait_slot_done(dve, s, i, n - 1)
                a = acc[1][:, :, :].rearrange("p t (h x d) -> p t h x d", h=2, x=2)
                for t in range(TT):
                    dve.tensor_copy(k_sb[:, t], a[:, t, :, 0])
                    ins = dve.tensor_copy(v_sb[:, t], a[:, t, :, 1])
                ins.then_inc(acc_free, 1)

            def att(g, s, i, j):
                kw = SEQ if g == 0 else P
                for h in range(QUAD):
                    head = g * QUAD + h
                    n1 = at(i, NG * QUAD, head + 1)
                    if j == 3 * h + 4:
                        dve.wait_ge(do_ps, n1)
                        dve.tensor_copy(o_sb[:, g, :, h, :], bD[:, (h % 2) * SEQ:(h % 2 + 1) * SEQ].rearrange(
                            "p (t d) -> p t d", t=TT)).then_inc(do_ready, 1)
                for h in range(QUAD):
                    head = g * QUAD + h
                    n1 = at(i, NG * QUAD, head + 1)
                    if j == 3 * h + 1:
                        dve.wait_ge(dscores, n1)
                        dve.wait_ge(bias_loaded[head % 2], at(i, bias_arrivals(NG * QUAD - 2 + head % 2), bias_arrivals(head)))
                        y = s_sb[:, 0:TT * kw].rearrange("p (t k) -> p t k", t=TT)
                        if g == 0:
                            b = bias_sb[:, h % 2, :].rearrange("p (t k) -> p t k", t=TT)
                        else:
                            b = bias_sb[:, h % 2, 0:P].rearrange("p (a k) -> p a k", a=1).broadcast_to([P, TT, P])
                        steps.done(dve.scalar_tensor_tensor(
                            out=y, in0=BK[h % 2][:, 0:TT * kw].rearrange("p (t k) -> p t k", t=TT),
                            scalar=DS_SCALE, in1=b, op0=ALU.mult, op1=ALU.add))
                        steps.wait()
                        m = m_sb[:, g, :].rearrange("p (t h) -> p t h", t=TT)[:, :, h]
                        steps.done(dve.tensor_reduce(m, y, AX.X, ALU.max))
                        steps.wait()
                        dve.tensor_scalar(stat[:, 8:10], m, -1.0, None, ALU.mult).then_inc(dnegmax, 1)

            def side(s, i, c, ci, j, n):
                prev = acc[(s.chunk0 + ci - 1) % 2]
                free1 = chunk_index(s, i, ci)
                if c.side == "hT":
                    if j in (1, 4):
                        z_block(2 if j == 1 else 3)
                    if 0 < j and j + 2 < KT // 2:
                        hT_pair(j + 2)
                elif c.side == "kva0":
                    half = (KV_RANK + ROPE) // 2
                    if j == 0:
                        evacuate(s, i, n, [(kva_sb[:, :, 0:half], prev[:, :, 0:half])])
                elif c.side == "kva1":
                    half = (KV_RANK + ROPE) // 2
                    if j == 0:
                        evacuate(s, i, n, [(kva_sb[:, :, half:2 * half], prev[:, :, 0:half])])
                    if j in (3, 4, 5):
                        scale_latent(kva_sb, KV_RANK, 1, j - 3)
                    if j in (6, 7):
                        norm_split(kva_hi, kva_lo, j - 6, j - 6)
                    if j == 8:
                        dve.wait_ge(kpe_hi_ready, 1)
                        dve.tensor_tensor(kpeT[ROPE:P, :], bC[0:ROPE, 0:SEQ], kpeT[0:ROPE, :].bitcast(F32),
                                          ALU.subtract).then_inc(kpe_lo_ready, 1)
                elif c.side == "qa0":
                    if j == 0:
                        evacuate(s, i, n, [(qa_sb[:, :, 0:CW], prev[:, :, :])])
                    if j == 2:
                        half = (ROWLEN + 1) // 2
                        dve.wait_ge(rows_ps, 1)
                        dve.tensor_copy(rowsb[:, half:ROWLEN], bB[0:NG * GH, 0:ROWLEN - half]).then_inc(rows_ready2, 1)
                elif c.side == "qa1":
                    if j == 0:
                        evacuate(s, i, n, [(qa_sb[:, :, CW:2 * CW], prev[:, :, :])])
                    if j in (3, 4, 5):
                        scale_latent(qa_sb, Q_RANK, 2, j - 3)
                    if 6 <= j < 10:
                        if j == 6:
                            dve.wait_ge(rows_stored, 16 * NG * GH)
                        norm_split(qa_hi, qa_lo, j - 6, j - 4)
                elif c.side in ("gm0", "gm1", "gm2", "gm3") and j == 0:
                    k = int(c.side[2])
                    silu(gm_sb[:, :, k * CW:(k + 1) * CW], prev[:, :, :], k + 1)
                elif c.side == "gm3_kv" and j == 0:
                    evacuate_q(s, i, n)
                elif c.side in ("mla", "mla_kv", "mla_last"):
                    step = j + 4 if c.side == "mla_kv" else j
                    if j == 0 and c.side != "mla_kv":
                        evacuate_kv(s, i, n)
                    unit = i if i is not None else MLA_HEADS // 2 - (1 if c.side == "mla_last" else 2)
                    cols = lambda first, w: bass.ds(i * 2 * w + first, w) if i is not None \
                        else slice(unit * 2 * w + first, unit * 2 * w + first + w)
                    heads = bass.ds(i * 2, 2) if i is not None else slice(2 * unit, 2 * unit + 2)
                    mla_side(step, unit + 1, unit * 2 + 1, lambda t, hh: gm_sb[:, t, cols(hh * HD, HD)],
                             am_hi[:, heads, :], am_lo[:, heads, :])
                    if j == 1 and c.side == "mla_kv":
                        evacuate_q(s, i, n - 1)
                elif c.side[:2] in ("qT", "kT"):
                    g = int(c.side[2])
                    e = 2 * g + (c.side[0] == "k")
                    if j == 0:
                        evacuate(s, i, n, [(a_sb, prev[:, :, :])])
                    if j == 2:
                        dst = dqT if c.side[0] == "q" else dkT
                        dve.wait_ge(dT_ps, at(i, 4 * NG, 2 * e + 2))
                        dve.tensor_copy(dst[:, 2:4, :], bB[:, :].rearrange("p (a b) -> p a b", a=2)).then_inc(dTB_ready, 1)
                elif c.side[:3] == "att":
                    if j == 0:
                        evacuate(s, i, n, [(dv_sb, prev[:, :, :])])
                    att(int(c.side[3]), s, i, j)
                elif c.side == "mix":
                    merge_groups(s, i, j, prev)
                elif c.side in ("rm", "rd", "rd_split"):
                    if j == 0:
                        dve.wait_ge(r_sig, at(i, 2, (1 if c.side == "rm" else 2) + (0 if i is not None else 14)))
                        dve.sem_inc(acc_free, 1)
                    elif c.side == "rd_split":
                        if j == 1:
                            dve.wait_ge(slot_done, s.slot0 + KT // 2)
                        for b in (2 * (j - 1), 2 * (j - 1) + 1):
                            dve.wait_ge(m_hi, b + 1)
                            dve.tensor_tensor(oper_lo[:, 2 * b:2 * b + 2, :], mT[:, 2 * b:2 * b + 2, :],
                                              oper_hi[:, 2 * b:2 * b + 2, :].bitcast(F32), ALU.subtract).then_inc(m_lo, 1)
                elif c.side == "ym" and j == 0:
                    wait_slot_done(dve, s, i, n - 1)
                    dve.tensor_tensor(ym, prev[:, :, :], sig_m, ALU.mult).then_inc(acc_free, 1)
                elif c.side in ("yd", "yd_last"):
                    if j == 0:
                        wait_slot_done(dve, s, i, n - 1)
                        dve.tensor_tensor(sig_d, prev[:, :, :], sig_d, ALU.mult).then_inc(acc_free, 1)
                        dve.wait_ge(acc_free, free1)
                        dve.tensor_tensor(ym, ym, sig_d, ALU.add).then_inc(merged, 1)
                    if c.side == "yd" and j == 3:
                        dve.wait_ge(mT_ps, at(i, 2, 2))
                        dve.tensor_copy(mT[:, bass.ds(i * 4 + 2, 2), :], bB[:, :].rearrange("p (a b) -> p a b", a=2)).then_inc(mTB_ready, 1)
                    if c.side == "yd_last" and j in (2, 3):
                        k = 28 + 2 * (j - 2)
                        dve.wait_ge(m_hi, 13 + j)
                        dve.tensor_tensor(oper_lo[:, k:k + 2, :], BK[j - 2][:, :].rearrange("p (a b) -> p a b", a=2),
                                          oper_hi[:, k:k + 2, :].bitcast(F32), ALU.subtract).then_inc(m_lo, 1)
                elif c.side[:3] == "fin" and j == 3:
                    residual(s, i, n - j, int(c.side[3]), prev)

            def residual(s, i, n, block0, prev):
                dve.wait_ge(slot_done, at(i, s.per_slot, s.slot0 + n))
                blocks = SEC["out"].per_chunk
                dve.wait_ge(h_again[block0 % 2], at(i, 16, 16 * (block0 // 2 + 1)))
                cols = bass.ds(i * (blocks * CW) + block0 * CW, CW) if i is not None else slice(block0 * CW, (block0 + 1) * CW)
                y = resid[:, :, cols]
                dve.scalar_tensor_tensor(out=y, in0=y, scalar=ALPHA, in1=prev[:, :, :], op0=ALU.mult,
                                         op1=ALU.add).then_inc(acc_free, 1)
                dve.wait_ge(acc_free, at(i, blocks, SEC["out0"].chunk0 + block0 + 1))
                part = bass.ds(i * blocks + block0, 1) if i is not None else slice(block0, block0 + 1)
                for t in range(TT):
                    ins = dve.bn_stats(ybn[:, t, part, :].rearrange("p a b -> p (a b)"), resid[:, t, cols])
                steps.done(ins)

            def merge_groups(s, i, j, prev):
                if j == 0:
                    silu(gate_sb[:, :, :], prev[:, :, :], at(i, 1, 5))
                    steps.done(dve.tensor_tensor(big_m, m_sb[:, 0], m_sb[:, 1], ALU.max))
                    steps.wait()
                    steps.done(dve.tensor_tensor(big_m, big_m, m_sb[:, 2], ALU.max))
                    steps.wait()
                    for g in range(NG):
                        ins = dve.tensor_tensor(wgt[:, g], m_sb[:, g], big_m, ALU.subtract)
                    ins.then_inc(mdiff_ready, 1)
                elif j == 1:
                    dve.wait_ge(mexp_ready, at(i, 1, 1))
                    steps.done(dve.tensor_tensor(den_sb, den_sb, wgt, ALU.mult))
                    steps.wait()
                    steps.done(dve.tensor_tensor(big_m, den_sb[:, 0], den_sb[:, 1], ALU.add))
                    steps.wait()
                    steps.done(dve.tensor_tensor(big_m, big_m, den_sb[:, 2], ALU.add))
                    steps.wait()
                    steps.done(dve.reciprocal(big_m, big_m))
                    steps.wait()
                    for g in range(NG):
                        ins = dve.tensor_tensor(wgt[:, g], wgt[:, g], big_m, ALU.mult)
                    steps.done(ins)
                    steps.wait()
                elif j in (2, 3, 4):
                    g = j - 2
                    o = o_sb[:, g].rearrange("p t h d -> p (t h) d")
                    w = wgt[:, g].rearrange("p (a b) -> p a b", b=1).broadcast_to([P, TT * QUAD, HD])
                    steps.done(dve.tensor_tensor(o, o, w, ALU.mult))
                    steps.wait()
                elif j in (5, 6):
                    g = j - 4
                    steps.done(dve.tensor_tensor(o_sb[:, 0], o_sb[:, 0], o_sb[:, g], ALU.add))
                    steps.wait()
                elif j == 7:
                    dve.tensor_tensor(o_sb[:, 0], o_sb[:, 0], gate_sb.rearrange("p t (h d) -> p t h d", h=QUAD),
                                      ALU.mult).then_inc(mix_ready, 1)
                elif j in (8, 9):
                    dve.wait_ge(b_hi_ready, at(i, 2, j - 7))
                    heads = bass.ds(i * QUAD + 2 * (j - 8), 2)
                    dve.tensor_tensor(b_lo[:, heads, :], BK[j - 8][:, :].rearrange("p (a b) -> p a b", a=2),
                                      b_hi[:, heads, :].bitcast(F32), ALU.subtract).then_inc(b_lo_ready, 1)

            def z_block(n):
                W = D // 4
                for t in range(TT):
                    dve.tensor_scalar(x_sb[:, t, n * W:(n + 1) * W], x_sb[:, t, n * W:(n + 1) * W], stat[:, 4 + t:5 + t],
                                      stat[:, 6 + t:7 + t], ALU.subtract, ALU.mult).then_inc(z_ready, 1)

            for n in range(D // CW):
                dve.wait_ge(x_loaded[n * XPARTS * CW // D], 32)
                for t in range(TT):
                    ins = dve.bn_stats(bn[:, t, n, :], x_sb[:, t, n * CW:(n + 1) * CW])
            steps.done(ins)
            steps.wait()
            aggregate(bn)
            after_root(1)
            z_block(0)
            split_lo(SECTIONS[0], None, chunk_ahead(0, 0), 0)
            hT_pair(0)
            z_block(1)
            split_lo(SECTIONS[0], None, chunk_ahead(0, 1), 1)
            hT_pair(1)
            split_lo(SECTIONS[0], None, chunk_ahead(0, 2), 2)
            hT_pair(2)
            for si, s in enumerate(SECTIONS):
                with turns(nc, dve, s) as i:
                    steps.enter(i, VECTOR_STEPS.get(s.name, 0))
                    for c, ci, j, n in slots_of(s):
                        side(s, i, c, ci, j, n)
                        if chunk_ahead(si, n + AHEAD):
                            split_lo(s, i, chunk_ahead(si, n + AHEAD), n + AHEAD)
                    steps.leave(s.turns)
            last = D // CW - 1
            residual(SECTIONS[-1], None, KT // 2, last, acc[1])
            steps.wait()
            aggregate(ybn)
            after_root(4)
            steps.done(dve.tensor_tensor(stat[:, 8:10], stat[:, 4:6], stat[:, 6:8], ALU.mult))
            steps.wait()
            dve.tensor_scalar(stat[:, 8:10], stat[:, 8:10], -1.0, None, ALU.mult).then_inc(shift_ready, 1)
            dve.wait_ge(ln_rows, 16 * (D // CW))
            dve.wait_ge(ln_rows_b, 16 * (D // CW))
            for cols in END_VECTOR:
                for t in range(TT):
                    steps.done(dve.scalar_tensor_tensor(out=resid[:, t, cols], in0=resid[:, t, cols], scalar=stat[:, 4 + t:5 + t],
                                                        in1=ln_g_row[:, cols], op0=ALU.subtract, op1=ALU.mult))
                steps.wait()
                for t in range(TT):
                    ins = dve.scalar_tensor_tensor(out=resid[:, t, cols], in0=resid[:, t, cols], scalar=stat[:, 6 + t:7 + t],
                                                   in1=ln_b_row[:, cols], op0=ALU.mult, op1=ALU.add)
                ins.then_inc(y_done_v, 1)

        @block.gpsimd
        def _(pool):
            steps = Steps(pool, pool_step)

            def rotate(v, tmp, done, shape):
                half = ROPE // 2
                if shape is None:
                    cos, sin = rope_sb[:, 0], rope_sb[:, 1]
                    a, b = (slice(None),) * 2 + (slice(0, half),), (slice(None),) * 2 + (slice(half, ROPE),)
                else:
                    cos, sin = (rope_sb[:, n].rearrange("p t (a d) -> p t a d", a=1).broadcast_to(shape) for n in range(2))
                    a, b = (slice(None),) * 3 + (slice(0, half),), (slice(None),) * 3 + (slice(half, ROPE),)
                pool.tensor_tensor(tmp[a], v[b], sin[a], ALU.mult)
                steps.done(pool.tensor_tensor(tmp[b], v[a], sin[b], ALU.mult))
                steps.wait()
                steps.done(pool.tensor_tensor(v, v, cos, ALU.mult))
                steps.wait()
                pool.tensor_tensor(v, v, tmp, ALU.add).then_inc(done, 1)

            def load_bias(quad, head):
                g, h = head // QUAD, head % QUAD
                b = head % 2
                first = (g * GH + quad * QUAD + h) * LEN * PITCH
                n_before = quad * NG * QUAD + head
                if n_before >= 2:
                    pool.wait_ge(dnegmax, n_before - 1)
                for t in range(TT if g == 0 else 1):
                    n = RES if g == 0 else 2
                    for r in range(2):
                        dst = bias_sb[r * LEN:(r + 1) * LEN, b, t * SEQ:t * SEQ + n * LEN].rearrange("p (r k) -> p r k", r=n)
                        off = (RES - 1 - r - 2 * t) * NDL + LEN - 1
                        src = bass.AP(tensor=bias_rows_d.tensor, offset=first + off, ap=[[PITCH - 1, LEN], [NDL, n], [1, LEN]])
                        pool.dma_start(dst, src).then_inc(bias_loaded[b], 16)

            for k in range(KT):
                pool.wait_ge(hT_hi, k + 1)
                pool.tensor_tensor(oper_lo[:, k, :], h_val[:, k % 4, :], oper_hi[:, k, :].bitcast(F32),
                                   ALU.subtract).then_inc(hT_lo, 1)
            pool.wait_ge(hT_ps, KT // 2)

            def keep_h(n):
                cols = slice(n * CW, (n + 1) * CW)
                g, b = emb_rows[n % 2][:, 0, :], emb_rows[n % 2][:, 1, :]
                if n >= 2:
                    pool.wait_ge(h_done, n - 1)
                pool.dma_start(g, emb_g[cols].rearrange("(a n) -> a n", a=1).broadcast_to([P, CW])).then_inc(emb_loaded[n % 2], 16)
                pool.dma_start(b, emb_b[cols].rearrange("(a n) -> a n", a=1).broadcast_to([P, CW])).then_inc(emb_loaded[n % 2], 16)
                pool.wait_ge(emb_loaded[n % 2], 32 * (n // 2 + 1))
                for t in range(TT):
                    steps.done(pool.tensor_tensor(x_sb[:, t, cols], x_sb[:, t, cols], g, ALU.mult))
                steps.wait()
                for t in range(TT):
                    ins = pool.tensor_tensor(x_sb[:, t, cols], x_sb[:, t, cols], b, ALU.add)
                ins.then_inc(h_done, 1)
                pool.wait_ge(h_done, n + 1)
                pool.dma_start(h_kept[n], x_sb[:, :, cols]).then_inc(h_stored, 16)

            for n in range(D // CW):
                if n == 4:
                    pool.wait_ge(normed, 1)
                    rotate(kva_sb[:, :, KV_RANK:KV_RANK + ROPE], ropet, kpe_roped, None)
                pool.wait_ge(slot_done, (17, 22, 28, 36, 48, 58, 65, 72)[n])
                keep_h(n)
                if n == 1:
                    pool.wait_ge(rows_ready, 1)
                    pool.wait_ge(rows_ready2, 1)
                    pool.wait_ge(bias_in, 64)
                if 1 <= n <= 4:
                    for head in range(6 * (n - 1), 6 * n):
                        first, count = (0, ROWLEN) if head < GH else ((RES - 2) * NDL, 3 * NDL)
                        src = rowsb[head:head + 1, first:first + count].rearrange("p (a n) -> p a n", a=1)
                        pool.dma_start(bias_rows_d[head:head + 1, :, first:first + count],
                                       src.broadcast_to([1, LEN, count])).then_inc(rows_stored, 16)
            pool.wait_ge(rows_stored, 16 * NG * GH)
            shape = [P, TT, 2, ROPE]
            for n, (turns_, chunks0) in enumerate(((None, SEC["unit0"].chunk0 + 1), (6, SEC["mla"].chunk0 + 1), (None, SEC["mla7"].chunk0 + 1))):
                def one(i):
                    pool.wait_ge(acc_free, at(i, 2, chunks0))
                    rotate(q_sb[:, :, :, NOPE:QHD], qrope, q_roped, shape)
                if turns_ is None:
                    one(None)
                else:
                    with pool.Fori(0, turns_) as i:
                        steps.enter(i, POOL_STEPS["mla"])
                        one(i)
                    steps.leave(turns_)
            pool.wait_ge(am_lo_ready, MLA_HEADS // 2)
            for quad in range(GH // QUAD):
                for head in range(NG * QUAD):
                    load_bias(quad, head)

            first = SEC["out0"].slot0
            pool.wait_ge(m_lo, KT // 2 - 2)
            pool.wait_ge(h_stored, 16 * (D // CW))
            for n in range(D // CW):
                cols = slice(n * CW, (n + 1) * CW)
                pool.wait_ge(slot_done, first + (KT // 2) * n)
                pool.dma_start(resid[:, :, cols], h_kept[n]).then_inc(h_again[n % 2], 16)
                pool.wait_ge(slot_done, first + (KT // 2) * n + 3)
                pool.dma_start(ln_g_row[:, cols], ln_g[0:1, cols].broadcast_to([P, CW])).then_inc(ln_rows, 16)
                pool.wait_ge(slot_done, first + (KT // 2) * n + 5)
                pool.dma_start(ln_b_row[:, cols], ln_b[0:1, cols].broadcast_to([P, CW])).then_inc(ln_rows_b, 16)
            pool.wait_ge(ln_rows, 16 * (D // CW))
            pool.wait_ge(ln_rows_b, 16 * (D // CW))
            for a, cols in enumerate(END_POOL):
                pool.wait_ge(z_out, a + 1)
                for t in range(TT):
                    steps.done(pool.tensor_tensor(resid[:, t, cols], resid[:, t, cols], ln_g_row[:, cols], ALU.mult))
                steps.wait()
                for t in range(TT):
                    ins = pool.tensor_tensor(resid[:, t, cols], resid[:, t, cols], ln_b_row[:, cols], ALU.add)
                ins.then_inc(y_done_p, 1)


def kernel(x, emb_ln_g, emb_ln_b, rel_bias, w_in, q_a_norm_g, w_q_b, kv_a_norm_g, w_kv_b, w_o_mla, w_o_dswa, w_out,
           ln_g, ln_b):
    import concourse.bacc as bacc
    from concourse.bass_utils import run_bass_kernel_spmd as run

    nc = bacc.Bacc("TRN2", target_bir_lowering=False, num_devices=1)
    given = {"x": x, "emb_ln_g": emb_ln_g, "emb_ln_b": emb_ln_b, "rel_bias": rel_bias, "w_in": w_in,
             "q_a_norm_g": q_a_norm_g, "w_q_b": w_q_b, "kv_a_norm_g": kv_a_norm_g, "w_kv_b": w_kv_b,
             "w_o_mla": w_o_mla, "w_o_dswa": w_o_dswa, "w_out": w_out, "ln_g": ln_g, "ln_b": ln_b}
    arrays, args = {}, []
    for name, value in given.items():
        a = np.ascontiguousarray(value)
        arrays[f"in_{name}"] = a
        args.append(nc.dram_tensor(f"in_{name}", a.shape, mybir.dt.from_np(a.dtype), kind="ExternalInput").ap())
    out = nc.dram_tensor("out_h", (1, SEQ, D), F32, kind="ExternalOutput").ap()
    program(nc, *args, out)
    return run(nc, [arrays], core_ids=[0]).results[0]["out_h"]
```
